# Optimizing a Trainium2 kernel written in Bass

```python
import math
import jax
import jax.numpy as jnp
from jax import lax
import numpy as np

D_MODEL = 1024
BATCH = 1
SEQ = 512
DEPTH = 2

GRID_W = 64
CTX_LEN = 256
EPS = 1e-6
F32 = jnp.float32
N_EVEN = (DEPTH + 1) // 2
N_ODD = DEPTH // 2

SSD_HEADS = 16
SSD_HEAD_DIM = 64
SSD_INNER = SSD_HEADS * SSD_HEAD_DIM
SSD_GROUPS = 2
SSD_R = SSD_HEADS // SSD_GROUPS
SSD_STATE = 128
SSD_BC = SSD_GROUPS * SSD_STATE
SSD_CHUNK = 128
DT_MIN = 1e-3
DT_MAX = 1e-1
MLSTM_HEADS = 4
MLSTM_QK_DIM = 128
MLSTM_V_DIM = 256
MLSTM_QK = MLSTM_HEADS * MLSTM_QK_DIM
MLSTM_INNER = MLSTM_HEADS * MLSTM_V_DIM
MLSTM_CHUNK = 128
CONV_K = 3
CONV_CH = SSD_INNER + 2 * SSD_BC + 2 * MLSTM_QK
CONV_SPLITS = (SSD_INNER, SSD_BC, SSD_BC, MLSTM_QK, MLSTM_QK)
EVEN_SPLITS = (CONV_CH, SSD_INNER, MLSTM_INNER, MLSTM_INNER, 2 * SSD_HEADS, 2 * MLSTM_HEADS, 2 * MLSTM_HEADS)
EVEN_PROJ = sum(EVEN_SPLITS)
EVEN_MIX = SSD_INNER + MLSTM_INNER
ATT_HEAD_DIM = 64
SWA_HEADS = 8
SWA_KV_HEADS = 2
DENSE_HEADS = 8
DENSE_KV_HEADS = 2
WINDOW = 128
BLOCK = 128
ROPE_THETA = 10000.0
ROPE_AXIS_DIM = ATT_HEAD_DIM // 2
ODD_SPLITS = (SWA_HEADS * ATT_HEAD_DIM, SWA_KV_HEADS * ATT_HEAD_DIM, SWA_KV_HEADS * ATT_HEAD_DIM,
              DENSE_HEADS * ATT_HEAD_DIM, DENSE_KV_HEADS * ATT_HEAD_DIM, DENSE_KV_HEADS * ATT_HEAD_DIM)
ODD_PROJ = sum(ODD_SPLITS)
ODD_MIX = (SWA_HEADS + DENSE_HEADS) * ATT_HEAD_DIM
N_GROUPS = 4
EXPERTS_PER_GROUP = 4
EXPERT_FF = 256
TOP_K = 2

kernel_name = 'hybrid_ssd_mlstm_swa_dense_hmoe_prefix_dit'

def _split(t, sizes):
    cuts = [int(i) for i in np.cumsum(sizes)[:-1]]
    return jnp.split(t, cuts, axis=-1)

def rmsnorm(x, w):
    xf = x.astype(F32)
    y = xf * lax.rsqrt(jnp.mean(xf * xf, axis=-1, keepdims=True) + EPS)
    return (y * w.astype(F32)).astype(x.dtype)

def group_rmsnorm(x, w, groups):
    shp = x.shape
    xg = x.astype(F32).reshape(shp[:-1] + (groups, shp[-1] // groups))
    xg = xg * lax.rsqrt(jnp.mean(xg * xg, axis=-1, keepdims=True) + EPS)
    return xg.reshape(shp) * w.astype(F32)

def adaln(cond, w, b):
    m = cond @ w + b
    return [t[:, None, :] for t in jnp.split(m, 6, axis=-1)]

def modulate(h, shift, scale):
    return h * (1 + scale) + shift

def rope_tables(S):
    rows = S // GRID_W
    row = jnp.repeat(jnp.arange(rows), GRID_W).astype(F32)
    col = (jnp.arange(rows * GRID_W) % GRID_W).astype(F32)
    inv = ROPE_THETA ** (-jnp.arange(0, ROPE_AXIS_DIM, 2, dtype=F32) / ROPE_AXIS_DIM)
    ang = jnp.concatenate([row[:, None] * inv, col[:, None] * inv], axis=-1)
    return jnp.cos(ang), jnp.sin(ang)

def apply_rope(x, cos, sin):
    xp = x.astype(F32).reshape(x.shape[:-1] + (-1, 2))
    x1, x2 = xp[..., 0], xp[..., 1]
    cs, sn = cos[:, None, :], sin[:, None, :]
    out = jnp.stack([x1 * cs - x2 * sn, x1 * sn + x2 * cs], axis=-1)
    return out.reshape(x.shape).astype(x.dtype)

def dwconv(x, w, b):
    C = x.shape[-1]
    y = lax.conv_general_dilated(x, w.astype(x.dtype)[:, None, :], window_strides=(1,),
                                 padding=[(CONV_K // 2, CONV_K // 2)],
                                 dimension_numbers=('NWC', 'WIO', 'NWC'), feature_group_count=C)
    return y + b

def _flip(t):
    return jnp.flip(t, axis=1)

def ssd_scan(xs, dA, Bm, Cm, h0):
    b, L, g, r, p = xs.shape
    Q = SSD_CHUNK
    c = L // Q
    xs = xs.reshape(b, c, Q, g, r, p)
    Bm = Bm.reshape(b, c, Q, g, SSD_STATE)
    Cm = Cm.reshape(b, c, Q, g, SSD_STATE)
    a_cum = jnp.cumsum(jnp.moveaxis(dA.reshape(b, c, Q, g, r), 2, -1), axis=-1)
    causal = jnp.tril(jnp.ones((Q, Q), dtype=bool))
    seg = a_cum[..., :, None] - a_cum[..., None, :]
    Lmat = jnp.exp(jnp.where(causal, seg, -jnp.inf))
    CB = jnp.einsum('bclgn,bcsgn->bcgls', Cm, Bm)
    y_diag = jnp.einsum('bcgls,bcgrls,bcsgrp->bclgrp', CB, Lmat, xs)
    decay_to_end = jnp.exp(a_cum[..., -1:] - a_cum)
    chunk_states = jnp.einsum('bclgn,bcgrl,bclgrp->bcgrpn', Bm, decay_to_end, xs)
    chunk_decay = jnp.exp(a_cum[..., -1])

    def step(h, inp):
        s, d = inp
        return d[..., None, None] * h + s, h

    h_last, h_in = lax.scan(step, h0, (jnp.moveaxis(chunk_states, 1, 0), jnp.moveaxis(chunk_decay, 1, 0)))
    h_in = jnp.moveaxis(h_in, 0, 1)
    y_off = jnp.einsum('bclgn,bcgrpn,bcgrl->bclgrp', Cm, h_in, jnp.exp(a_cum))
    return (y_diag + y_off).reshape(b, L, g, r, p), h_last

def ssd_bidir(xs, Bm, Cm, dt_raw, dt_bias, a_log, d_skip, h0_f, h0_b):
    b, L, _ = xs.shape
    x = xs.reshape(b, L, SSD_GROUPS, SSD_R, SSD_HEAD_DIM)
    Bm = Bm.reshape(b, L, SSD_GROUPS, SSD_STATE)
    Cm = Cm.reshape(b, L, SSD_GROUPS, SSD_STATE)
    dt = jax.nn.softplus(dt_raw.reshape(b, L, 2, SSD_HEADS) + dt_bias)
    dA = (dt * (-jnp.exp(a_log))).reshape(b, L, 2, SSD_GROUPS, SSD_R)
    dtg = dt.reshape(b, L, 2, SSD_GROUPS, SSD_R)
    y_f, hf = ssd_scan(x * dtg[:, :, 0, :, :, None], dA[:, :, 0], Bm, Cm, h0_f)
    y_b, hb = ssd_scan(_flip(x * dtg[:, :, 1, :, :, None]), _flip(dA[:, :, 1]), _flip(Bm), _flip(Cm), h0_b)
    y = y_f + _flip(y_b) + x * d_skip.reshape(SSD_GROUPS, SSD_R)[..., None]
    return y.reshape(b, L, SSD_INNER), hf, hb

def mlstm_scan(q, k, v, ig, lf, state):
    b, L, H, dk = q.shape
    dv = v.shape[-1]
    Q = MLSTM_CHUNK
    c = L // Q
    q = q.reshape(b, c, Q, H, dk)
    k = k.reshape(b, c, Q, H, dk)
    v = v.reshape(b, c, Q, H, dv)
    ig = jnp.moveaxis(ig.reshape(b, c, Q, H), 2, -1)
    bcum = jnp.cumsum(jnp.moveaxis(lf.reshape(b, c, Q, H), 2, -1), axis=-1)
    causal = jnp.tril(jnp.ones((Q, Q), dtype=bool))
    Dlog = jnp.where(causal, bcum[..., :, None] - bcum[..., None, :] + ig[..., None, :], -jnp.inf)
    w_end = bcum[..., -1:] - bcum + ig
    m_loc = jnp.max(w_end, axis=-1)
    e_end = jnp.exp(w_end - m_loc[..., None])
    C_loc = jnp.einsum('bchs,bcshk,bcshv->bchkv', e_end, k, v)
    n_loc = jnp.einsum('bchs,bcshk->bchk', e_end, k)
    f_chunk = bcum[..., -1]

    def step(carry, inp):
        C, n, m = carry
        Cl, nl, ml, fc = inp
        m_new = jnp.maximum(fc + m, ml)
        a = jnp.exp(fc + m - m_new)
        bb = jnp.exp(ml - m_new)
        C_new = a[..., None, None] * C + bb[..., None, None] * Cl
        n_new = a[..., None] * n + bb[..., None] * nl
        return (C_new, n_new, m_new), (C, n, m)

    final, (C_in, n_in, m_in) = lax.scan(
        step, state,
        (jnp.moveaxis(C_loc, 1, 0), jnp.moveaxis(n_loc, 1, 0), jnp.moveaxis(m_loc, 1, 0), jnp.moveaxis(f_chunk, 1, 0)))
    C_in = jnp.moveaxis(C_in, 0, 1)
    n_in = jnp.moveaxis(n_in, 0, 1)
    m_in = jnp.moveaxis(m_in, 0, 1)
    m_inter = bcum + m_in[..., None]
    m_t = jnp.maximum(m_inter, jnp.max(Dlog, axis=-1))
    P = jnp.exp(Dlog - m_t[..., None]) * jnp.einsum('bclhk,bcshk->bchls', q, k)
    w_inter = jnp.exp(m_inter - m_t)
    num = jnp.einsum('bchls,bcshv->bclhv', P, v) + jnp.einsum('bchl,bclhk,bchkv->bclhv', w_inter, q, C_in)
    den = jnp.sum(P, axis=-1) + w_inter * jnp.einsum('bclhk,bchk->bchl', q, n_in)
    den = jnp.maximum(jnp.abs(den), jnp.exp(-m_t))
    h = num / jnp.moveaxis(den, -1, 2)[..., None]
    return h.reshape(b, L, H, dv), final

def mlstm_bidir(q, k, v, ig_raw, fg_raw, ig_bias, fg_bias, st_f, st_b):
    b, L = q.shape[:2]
    ig = ig_raw.reshape(b, L, 2, MLSTM_HEADS) + ig_bias
    lf = jax.nn.log_sigmoid(fg_raw.reshape(b, L, 2, MLSTM_HEADS) + fg_bias)
    h_f, sf = mlstm_scan(q, k, v, ig[:, :, 0], lf[:, :, 0], st_f)
    h_b, sb = mlstm_scan(_flip(q), _flip(k), _flip(v), _flip(ig[:, :, 1]), _flip(lf[:, :, 1]), st_b)
    return h_f + _flip(h_b), sf, sb

def zero_states(b):
    h0 = jnp.zeros((b, SSD_GROUPS, SSD_R, SSD_HEAD_DIM, SSD_STATE), F32)
    st = (jnp.zeros((b, MLSTM_HEADS, MLSTM_QK_DIM, MLSTM_V_DIM), F32),
          jnp.zeros((b, MLSTM_HEADS, MLSTM_QK_DIM), F32),
          jnp.zeros((b, MLSTM_HEADS), F32))
    return (h0, h0, st, st)

def recurrent_heads(u, conv_w, conv_b, dt_bias, a_log, d_skip, ssd_norm_w, ig_bias, fg_bias, mlstm_norm_w, init):
    b, L, _ = u.shape
    conv_in, z, v, o, dt_raw, ig_raw, fg_raw = _split(u, EVEN_SPLITS)
    conv_out = jax.nn.silu(dwconv(conv_in, conv_w, conv_b)).astype(F32)
    xs, Bm, Cm, q, k = _split(conv_out, CONV_SPLITS)
    h0_f, h0_b, st_f, st_b = init
    y_ssd, hf, hb = ssd_bidir(xs, Bm, Cm, dt_raw.astype(F32), dt_bias, a_log, d_skip, h0_f, h0_b)
    y_ssd = group_rmsnorm(y_ssd * jax.nn.silu(z.astype(F32)), ssd_norm_w, SSD_GROUPS)
    hm, sf, sb = mlstm_bidir(q.reshape(b, L, MLSTM_HEADS, MLSTM_QK_DIM),
                             k.reshape(b, L, MLSTM_HEADS, MLSTM_QK_DIM) * (MLSTM_QK_DIM ** -0.5),
                             v.astype(F32).reshape(b, L, MLSTM_HEADS, MLSTM_V_DIM),
                             ig_raw.astype(F32), fg_raw.astype(F32), ig_bias, fg_bias, st_f, st_b)
    hm = group_rmsnorm(hm.reshape(b, L, MLSTM_INNER), mlstm_norm_w, MLSTM_HEADS) * jax.nn.sigmoid(o.astype(F32))
    return jnp.concatenate([y_ssd, hm], axis=-1), (hf, hb, sf, sb)

def recurrent_mixer(a_ctx, a_lat, w_in, conv_w, conv_b, dt_bias, a_log, d_skip, ssd_norm_w, ig_bias, fg_bias,
                    mlstm_norm_w, w_out):
    y_ctx, finals = recurrent_heads(a_ctx @ w_in, conv_w, conv_b, dt_bias, a_log, d_skip, ssd_norm_w, ig_bias,
                                    fg_bias, mlstm_norm_w, zero_states(a_ctx.shape[0]))
    y_lat, _ = recurrent_heads(a_lat @ w_in, conv_w, conv_b, dt_bias, a_log, d_skip, ssd_norm_w, ig_bias,
                               fg_bias, mlstm_norm_w, finals)
    return y_ctx.astype(a_ctx.dtype) @ w_out, y_lat.astype(a_lat.dtype) @ w_out

def full_attention(q, k, v, sink):
    b, T, H, dh = q.shape
    KV = k.shape[2]
    G = H // KV
    s = jnp.einsum('bqkgd,btkd->bkgqt', q.reshape(b, T, KV, G, dh), k).astype(F32) * (dh ** -0.5)
    if sink is not None:
        sk = jnp.broadcast_to(sink.astype(F32).reshape(KV, G, 1, 1), s.shape[:-1] + (1,))
        p = jax.nn.softmax(jnp.concatenate([sk, s], axis=-1), axis=-1)[..., 1:]
    else:
        p = jax.nn.softmax(s, axis=-1)
    o = jnp.einsum('bkgqt,btkd->bqkgd', p.astype(v.dtype), v)
    return o.reshape(b, T, H * dh)

def window_attention(q, k, v, k_ctx, v_ctx, sink):
    b, S, H, dh = q.shape
    KV = k.shape[2]
    G = H // KV
    T = k_ctx.shape[1]
    nb = S // BLOCK
    qg = q.reshape(b, S, KV, G, dh)
    pad = ((0, 0), (BLOCK, BLOCK), (0, 0), (0, 0))
    kp = jnp.pad(k, pad)
    vp = jnp.pad(v, pad)
    scale = dh ** -0.5
    qpos = BLOCK + jnp.arange(BLOCK)
    kpos = jnp.arange(3 * BLOCK)
    in_window = jnp.abs(kpos[None, :] - qpos[:, None]) <= WINDOW
    sink_logit = sink.astype(F32).reshape(KV, G, 1, 1)

    def one_block(j):
        start = j * BLOCK
        qb = lax.dynamic_slice_in_dim(qg, start, BLOCK, axis=1)
        kb = lax.dynamic_slice_in_dim(kp, start, 3 * BLOCK, axis=1)
        vb = lax.dynamic_slice_in_dim(vp, start, 3 * BLOCK, axis=1)
        kabs = start - BLOCK + kpos
        valid = in_window & ((kabs >= 0) & (kabs < S))[None, :]
        s_loc = jnp.where(valid, jnp.einsum('bqkgd,bskd->bkgqs', qb, kb).astype(F32) * scale, -jnp.inf)
        s_ctx = jnp.einsum('bqkgd,btkd->bkgqt', qb, k_ctx).astype(F32) * scale
        s_sink = jnp.broadcast_to(sink_logit, s_ctx.shape[:-1] + (1,))
        p = jax.nn.softmax(jnp.concatenate([s_sink, s_ctx, s_loc], axis=-1), axis=-1).astype(v.dtype)
        return (jnp.einsum('bkgqt,btkd->bqkgd', p[..., 1:1 + T], v_ctx)
                + jnp.einsum('bkgqs,bskd->bqkgd', p[..., 1 + T:], vb))

    out = lax.map(one_block, jnp.arange(nb))
    return jnp.moveaxis(out, 0, 1).reshape(b, S, H * dh)

def dense_block_attention(q, k_all, v_all):
    b, S, H, dh = q.shape
    KV = k_all.shape[2]
    G = H // KV
    nb = S // BLOCK
    qb = jnp.moveaxis(q.reshape(b, nb, BLOCK, KV, G, dh), 1, 0)

    def one_block(qblk):
        s = jnp.einsum('bqkgd,btkd->bkgqt', qblk, k_all).astype(F32) * (dh ** -0.5)
        p = jax.nn.softmax(s, axis=-1).astype(v_all.dtype)
        return jnp.einsum('bkgqt,btkd->bqkgd', p, v_all)

    out = lax.map(one_block, qb)
    return jnp.moveaxis(out, 0, 1).reshape(b, S, H * dh)

def attention_mixer(a_ctx, a_lat, w_in, sink, q_norm_w, k_norm_w, w_out, cos, sin, need_ctx):
    def project(a):
        b, L, _ = a.shape
        qs, ks, vs, qd, kd, vd = _split(a @ w_in, ODD_SPLITS)
        hd = lambda t, n: t.reshape(b, L, n, ATT_HEAD_DIM)
        return (hd(qs, SWA_HEADS), hd(ks, SWA_KV_HEADS), hd(vs, SWA_KV_HEADS),
                rmsnorm(hd(qd, DENSE_HEADS), q_norm_w), rmsnorm(hd(kd, DENSE_KV_HEADS), k_norm_w),
                hd(vd, DENSE_KV_HEADS))

    qs_c, ks_c, vs_c, qd_c, kd_c, vd_c = project(a_ctx)
    qs_l, ks_l, vs_l, qd_l, kd_l, vd_l = project(a_lat)
    rot = lambda t: apply_rope(t, cos, sin)
    y_swa = window_attention(rot(qs_l), rot(ks_l), vs_l, ks_c, vs_c, sink)
    y_den = dense_block_attention(rot(qd_l), jnp.concatenate([kd_c, rot(kd_l)], axis=1),
                                  jnp.concatenate([vd_c, vd_l], axis=1))
    y_lat = jnp.concatenate([y_swa, y_den], axis=-1) @ w_out
    y_ctx = None
    if need_ctx:
        y_ctx = jnp.concatenate([full_attention(qs_c, ks_c, vs_c, sink),
                                 full_attention(qd_c, kd_c, vd_c, None)], axis=-1) @ w_out
    return y_ctx, y_lat

def hier_moe(h, w_group, w_expert, w_gate, w_up, w_down):
    b, L, Dm = h.shape
    t = h.reshape(b * L, Dm)
    p_group = jax.nn.softmax((t @ w_group).astype(F32), axis=-1)
    p_top, g_idx = lax.top_k(p_group, 1)
    e_logits = (t @ w_expert).astype(F32).reshape(-1, N_GROUPS, EXPERTS_PER_GROUP)
    e_sel = jnp.take_along_axis(e_logits, g_idx[:, :, None], axis=1)[:, 0]
    w_top, e_idx = lax.top_k(jax.nn.softmax(e_sel, axis=-1), TOP_K)
    w_top = w_top / jnp.sum(w_top, axis=-1, keepdims=True) * p_top
    gate_in_group = jnp.sum(jax.nn.one_hot(e_idx, EXPERTS_PER_GROUP, dtype=F32) * w_top[..., None], axis=1)
    gates = (jax.nn.one_hot(g_idx[:, 0], N_GROUPS, dtype=F32)[:, :, None] * gate_in_group[:, None, :]).astype(t.dtype)
    out = jnp.zeros_like(t)
    for g in range(N_GROUPS):
        a = jnp.einsum('nd,edf->nef', t, w_gate[g])
        u = jnp.einsum('nd,edf->nef', t, w_up[g])
        hid = jax.nn.silu(a) * u * gates[:, g, :, None]
        out = out + jnp.einsum('nef,efd->nd', hid, w_down[g])
    return out.reshape(b, L, Dm)

def setup_inputs(seed: int = 0) -> dict:
    key = jax.random.key(seed)
    ks = jax.random.split(key, 32)
    nrm = lambda k, shape, s: jax.random.normal(k, shape, F32) * s
    gain = lambda k, shape: 1.0 + 0.05 * jax.random.normal(k, shape, F32)
    dt0 = jnp.exp(jax.random.uniform(ks[11], (N_EVEN, 2, SSD_HEADS), F32, math.log(DT_MIN), math.log(DT_MAX)))
    return {
        'x': nrm(ks[0], (BATCH, SEQ, D_MODEL), 1.0),
        'c': nrm(ks[1], (BATCH, D_MODEL), 1.0),
        'ctx': nrm(ks[2], (BATCH, CTX_LEN, D_MODEL), 1.0),
        'c_ctx': nrm(ks[3], (D_MODEL,), 1.0),
        'ada_w': nrm(ks[4], (DEPTH, D_MODEL, 6 * D_MODEL), 0.5 * D_MODEL ** -0.5),
        'ada_b': nrm(ks[5], (DEPTH, 6 * D_MODEL), 0.02),
        'norm1_w': gain(ks[6], (DEPTH, D_MODEL)),
        'norm2_w': gain(ks[7], (DEPTH, D_MODEL)),
        'ev_w_in': nrm(ks[8], (N_EVEN, D_MODEL, EVEN_PROJ), D_MODEL ** -0.5),
        'ev_conv_w': nrm(ks[9], (N_EVEN, CONV_K, CONV_CH), CONV_K ** -0.5),
        'ev_conv_b': nrm(ks[10], (N_EVEN, CONV_CH), 0.02),
        'ev_dt_bias': dt0 + jnp.log(-jnp.expm1(-dt0)),
        'ev_a_log': jnp.log(jax.random.uniform(ks[12], (N_EVEN, 2, SSD_HEADS), F32, 1.0, 16.0)),
        'ev_d_skip': gain(ks[13], (N_EVEN, SSD_HEADS)),
        'ev_ssd_norm_w': gain(ks[14], (N_EVEN, SSD_INNER)),
        'ev_ig_bias': nrm(ks[15], (N_EVEN, 2, MLSTM_HEADS), 0.1),
        'ev_fg_bias': jax.random.uniform(ks[16], (N_EVEN, 2, MLSTM_HEADS), F32, 3.0, 6.0),
        'ev_mlstm_norm_w': gain(ks[17], (N_EVEN, MLSTM_INNER)),
        'ev_w_out': nrm(ks[18], (N_EVEN, EVEN_MIX, D_MODEL), EVEN_MIX ** -0.5),
        'od_w_in': nrm(ks[19], (N_ODD, D_MODEL, ODD_PROJ), D_MODEL ** -0.5),
        'od_sink': nrm(ks[20], (N_ODD, SWA_HEADS), 0.5),
        'od_q_norm_w': gain(ks[21], (N_ODD, ATT_HEAD_DIM)),
        'od_k_norm_w': gain(ks[22], (N_ODD, ATT_HEAD_DIM)),
        'od_w_out': nrm(ks[23], (N_ODD, ODD_MIX, D_MODEL), ODD_MIX ** -0.5),
        'moe_w_group': nrm(ks[24], (DEPTH, D_MODEL, N_GROUPS), D_MODEL ** -0.5),
        'moe_w_expert': nrm(ks[25], (DEPTH, D_MODEL, N_GROUPS * EXPERTS_PER_GROUP), D_MODEL ** -0.5),
        'moe_w_gate': nrm(ks[26], (DEPTH, N_GROUPS, EXPERTS_PER_GROUP, D_MODEL, EXPERT_FF), D_MODEL ** -0.5),
        'moe_w_up': nrm(ks[27], (DEPTH, N_GROUPS, EXPERTS_PER_GROUP, D_MODEL, EXPERT_FF), D_MODEL ** -0.5),
        'moe_w_down': nrm(ks[28], (DEPTH, N_GROUPS, EXPERTS_PER_GROUP, EXPERT_FF, D_MODEL), EXPERT_FF ** -0.5),
        'final_norm_w': gain(ks[29], (D_MODEL,)),
    }

def reference(x, c, ctx, c_ctx, ada_w, ada_b, norm1_w, norm2_w,
              ev_w_in, ev_conv_w, ev_conv_b, ev_dt_bias, ev_a_log, ev_d_skip, ev_ssd_norm_w,
              ev_ig_bias, ev_fg_bias, ev_mlstm_norm_w, ev_w_out,
              od_w_in, od_sink, od_q_norm_w, od_k_norm_w, od_w_out,
              moe_w_group, moe_w_expert, moe_w_gate, moe_w_up, moe_w_down, final_norm_w):
    S = x.shape[1]
    cos, sin = rope_tables(S)
    silu_c = jax.nn.silu(c)
    silu_cc = jax.nn.silu(c_ctx)[None]
    h_lat, h_ctx = x, ctx
    for layer in range(DEPTH):
        li = layer // 2
        need_ctx = layer < DEPTH - 1
        sh1, sc1, g1, sh2, sc2, g2 = adaln(silu_c, ada_w[layer], ada_b[layer])
        csh1, csc1, cg1, csh2, csc2, cg2 = adaln(silu_cc, ada_w[layer], ada_b[layer])
        a_lat = modulate(rmsnorm(h_lat, norm1_w[layer]), sh1, sc1)
        a_ctx = modulate(rmsnorm(h_ctx, norm1_w[layer]), csh1, csc1)
        if layer % 2 == 0:
            y_ctx, y_lat = recurrent_mixer(a_ctx, a_lat, ev_w_in[li], ev_conv_w[li], ev_conv_b[li], ev_dt_bias[li],
                                           ev_a_log[li], ev_d_skip[li], ev_ssd_norm_w[li], ev_ig_bias[li],
                                           ev_fg_bias[li], ev_mlstm_norm_w[li], ev_w_out[li])
        else:
            y_ctx, y_lat = attention_mixer(a_ctx, a_lat, od_w_in[li], od_sink[li], od_q_norm_w[li],
                                           od_k_norm_w[li], od_w_out[li], cos, sin, need_ctx)
        h_lat = h_lat + g1 * y_lat
        f_lat = hier_moe(modulate(rmsnorm(h_lat, norm2_w[layer]), sh2, sc2), moe_w_group[layer],
                         moe_w_expert[layer], moe_w_gate[layer], moe_w_up[layer], moe_w_down[layer])
        h_lat = h_lat + g2 * f_lat
        if need_ctx:
            h_ctx = h_ctx + cg1 * y_ctx
            f_ctx = hier_moe(modulate(rmsnorm(h_ctx, norm2_w[layer]), csh2, csc2), moe_w_group[layer],
                             moe_w_expert[layer], moe_w_gate[layer], moe_w_up[layer], moe_w_down[layer])
            h_ctx = h_ctx + cg2 * f_ctx
    return rmsnorm(h_lat, final_norm_w)


_drawn_inputs = setup_inputs


def setup_inputs(seed=0):
    import zlib

    import numpy as np

    out = dict(_drawn_inputs(seed))
    spreads = {}
    factors = {'norm1_w': 2.719,
     'ev_conv_b': 5.649,
     'ev_d_skip': 48.758,
     'ev_ssd_norm_w': 3.793,
     'ev_ig_bias': 64.0,
     'ev_mlstm_norm_w': 8.0,
     'od_sink': 64.0,
     'od_q_norm_w': 8.0,
     'od_k_norm_w': 8.0}
    for name, (base, spread) in spreads.items():
        noise = np.random.default_rng([zlib.crc32(name.encode()), seed]).standard_normal(out[name].shape)
        drawn = base * np.exp(spread * noise) if base else spread * noise
        out[name] = jnp.asarray(drawn.astype(out[name].dtype))
    for name, factor in factors.items():
        out[name] = (out[name] * factor).astype(out[name].dtype)
    return out
```

```python
from contextlib import ExitStack

import numpy as np

import concourse.bass as bass
from concourse import mybir
from concourse.alu_op_type import AluOpType as ALU

F32 = mybir.dt.float32
BF16 = mybir.dt.bfloat16
I32 = mybir.dt.int32
ACT = mybir.ActivationFunctionType
AX = mybir.AxisListType

P = 128
D = 1024
KD = D // P
DEPTH = 2
CTX, SEQ = 256, 512
TOK = CTX + SEQ
NT = TOK // P
CT = CTX // P
EPS = 1e-6
BANK = 512

SSD_HEADS, SSD_P, SSD_GROUPS, SSD_STATE = 16, 64, 2, 128
ML_HEADS, ML_QK, ML_V = 4, 128, 256
CONV_CH = 2560
NCH = CONV_CH // P
ZVO = 3 * 1024
TAIL0 = CONV_CH + ZVO
TAIL = 48
NDT, NML = 2 * SSD_HEADS, 2 * ML_HEADS

COL_W, COL_B, COL_N1, COL_SSD, COL_ML, NCOL = 0, 3 * NCH, 4 * NCH, 4 * NCH + 16, 4 * NCH + 24, 4 * NCH + 32
C_ID, C_GE, C_LE, C_NGE, C_NLE, C_STRICT, C_ONE, C_FWD, NCONST = 0, 128, 256, 384, 512, 640, 768, 896, 900
NEG = -1e30


def wait_alone(eng, sem, value, passed):
    eng.wait_ge(sem, value)
    eng.sem_inc(passed, 1)


class Chain:

    def __init__(self, eng, sem):
        self.eng, self.sem, self.base, self.n = eng, sem, 0, 0

    def __call__(self, ins):
        self.n += 1
        ins.then_inc(self.sem, 1)
        self.eng.wait_ge(self.sem, self.base + self.n)

    def enter(self, i, per):
        self.start = self.base + self.n
        self.base, self.n, self.per = self.start + i * per, 0, per

    def leave(self, count):
        assert self.n == self.per, (self.n, self.per)
        self.base, self.n = self.start + count * self.per, 0


class Kit:

    def __init__(self, nc, A, out, stack):
        self.nc, self.A, self.out, self.stack = nc, A, out, stack
        self.nsem, self.sems = 0, []
        self.consts = self.keep("consts", [P, NCONST])
        self.pcol = self.keep("pcol", [P, NCOL])
        self.mcol = self.keep("mcol", [P, 2, DEPTH, 2, KD])
        self.scale1 = self.keep("scale1", [P, 2, DEPTH, KD])

    def sem(self, name):
        self.nsem += 1
        self.sems.append(self.nc.alloc_semaphore(name=f"{name}_{self.nsem}"))
        return self.sems[-1]

    def recycle(self):
        with self.nc.Block() as block:

            @block.gpsimd
            def _(pool):
                self.nc.clear_and_free_semaphores(self.sems)

        self.sems = []

    def dram(self, name, shape, dt=F32):
        return self.nc.dram_tensor(name, shape, dt).ap()

    def keep(self, name, shape, dt=F32):
        return self.stack.enter_context(self.nc.sbuf_tensor(name, shape, dt))


def phase_adaln(kit):
    nc, A = kit.nc, kit.A
    RING, W6 = 3, 6 * D
    ITER = W6 // BANK // RING
    with ExitStack() as st:
        sb = lambda n, s, d=F32: st.enter_context(nc.sbuf_tensor(n, s, d))
        crow = sb("ada_crow", [16, P])
        csil = sb("ada_csil", [16, P])
        ccol = sb("ada_ccol", [P, 16])
        bias = sb("ada_bias", [2, DEPTH * W6])
        rows = sb("ada_rows", [2, DEPTH * W6])
        ring = sb("ada_ring", [P, RING, KD, BANK])
        pt = st.enter_context(nc.psum_tensor("ada_pt", [P, BANK], F32))
        ps = [st.enter_context(nc.psum_tensor(f"ada_ps{s}", [P, BANK], F32)) for s in range(RING)]
        c_loaded, consts_loaded, silu_done, col_done, ccol_ready = (
            kit.sem(x) for x in ("c_loaded", "consts_loaded", "silu_done", "col_done", "ccol_ready"))
        w_loaded = [kit.sem(f"ada_w_loaded{s}") for s in range(RING)]
        w_free, mod_ready, bank_free, stored = (
            kit.sem(x) for x in ("ada_w_free", "ada_mod_ready", "ada_bank_free", "ada_stored"))
        consts = kit.consts
        w_view = [A["ada_w"][l].rearrange("(k p) n -> p k n", p=P) for l in range(DEPTH)]
        block = st.enter_context(nc.Block())

        @block.sync
        def _(sp):
            for cond, name in enumerate(("c", "c_ctx")):
                v = A[name]
                src = v.rearrange("a (k p) -> (a k) p", p=P) if cond == 0 else v.rearrange("(k p) -> k p", p=P)
                sp.dma_start(crow[8 * cond:8 * cond + 8, :], src).then_inc(c_loaded, 16)
            sp.dma_start(consts[:, :], A["consts"]).then_inc(consts_loaded, 16)
            sp.dma_start(bias[:, :], A["ada_b"].rearrange("l n -> (l n)").partition_broadcast(2)).then_inc(c_loaded, 16)
            for l in range(DEPTH):
                with sp.Fori(0, ITER) as i:
                    for s in range(RING):
                        sp.wait_ge(w_free, (l * ITER + i) * RING + s + 1)
                        sp.dma_start(ring[:, s], w_view[l][:, :, bass.ds((i * RING + s) * BANK, BANK)]).then_inc(w_loaded[s], 16)
            sp.wait_ge(bank_free, RING + DEPTH * ITER * RING)
            sp.dma_start(kit.mod, rows[:, :]).then_inc(stored, 16)
            sp.wait_ge(stored, 16)

        @block.scalar
        def _(act):
            act.wait_ge(c_loaded, 48)
            nc.scalar.activation(csil[:, :], crow[:, :], ACT.Silu).then_inc(silu_done, 1)
            act.wait_ge(col_done, 1)
            nc.scalar.copy(ccol[:, :], pt[:, 0:16]).then_inc(ccol_ready, 1)

        @block.tensor
        def _(pe):
            for _s in range(RING):
                pe.sem_inc(w_free, 1)
            pe.wait_ge(consts_loaded, 16)
            pe.wait_ge(silu_done, 1)
            nc.tensor.transpose(pt[:, 0:16], csil[:, :], consts[0:16, 0:16]).then_inc(col_done, 1)
            pe.wait_ge(ccol_ready, 1)
            for l in range(DEPTH):
                with pe.Fori(0, ITER) as i:
                    for s in range(RING):
                        pe.wait_ge(w_loaded[s], (l * ITER + i) * 16 + 16)
                        pe.wait_ge(bank_free, (l * ITER + i) * RING + s + 1)
                        for k in range(KD):
                            last = nc.tensor.matmul(ps[s][0:2, :], ccol[:, k:16:8], ring[:, s, k, :],
                                                    start=(k == 0), stop=(k == KD - 1))
                        last.then_inc(mod_ready, 1)
                        pe.wait_ge(mod_ready, (l * ITER + i) * RING + s + 1)
                        pe.sem_inc(w_free, 1)

        @block.vector
        def _(dve):
            for _s in range(RING):
                dve.sem_inc(bank_free, 1)
            dve.wait_ge(c_loaded, 48)
            for l in range(DEPTH):
                with dve.Fori(0, ITER) as i:
                    for s in range(RING):
                        dve.wait_ge(mod_ready, (l * ITER + i) * RING + s + 1)
                        at = l * W6 + (i * RING + s) * BANK
                        nc.vector.tensor_tensor(rows[:, bass.ds(at, BANK)], ps[s][0:2, :], bias[:, bass.ds(at, BANK)],
                                                ALU.add).then_inc(bank_free, 1)


def phase_columns(kit):
    nc, A, consts = kit.nc, kit.A, kit.consts
    with ExitStack() as st:
        sb = lambda n, s, d=F32: st.enter_context(nc.sbuf_tensor(n, s, d))
        prow, mrow = sb("prow", [NCOL, P]), sb("mrow", [64, P])
        pp = st.enter_context(nc.psum_tensor("col_pp", [P, BANK], F32))
        rows_loaded, turned, cols_ready, scaled = (kit.sem(x) for x in ("prow_loaded", "col_turned", "cols_ready", "scaled"))
        loads = [(prow[COL_W:COL_W + 3 * NCH, :], A["ev_conv_w"][0].rearrange("t (c p) -> (t c) p", p=P)),
                 (prow[COL_B:COL_B + NCH, :], A["ev_conv_b"][0].rearrange("(c p) -> c p", p=P)),
                 (prow[COL_N1:COL_N1 + 16, :], A["norm1_w"].rearrange("l (k p) -> (l k) p", p=P)),
                 (prow[COL_SSD:COL_SSD + 8, :], A["ev_ssd_norm_w"][0].rearrange("(k p) -> k p", p=P)),
                 (prow[COL_ML:COL_ML + 8, :], A["ev_mlstm_norm_w"][0].rearrange("(k p) -> k p", p=P))]
        for cond in range(2):
            for l in range(DEPTH):
                r = (cond * DEPTH + l) * 16
                loads.append((mrow[r:r + 16, :],
                              kit.mod[cond, l * 6 * D:l * 6 * D + 2 * D].rearrange("(k p) -> k p", p=P)))
        block = st.enter_context(nc.Block())

        @block.sync
        def _(sp):
            for dst, src in loads:
                sp.dma_start(dst, src).then_inc(rows_loaded, 16)

        @block.tensor
        def _(pe):
            pe.wait_ge(rows_loaded, 16 * len(loads))
            nc.tensor.transpose(pp[:, 0:NCOL], prow[:, :], consts[0:NCOL, 0:NCOL])
            nc.tensor.transpose(pp[:, 128:192], mrow[:, :], consts[0:64, 0:64]).then_inc(turned, 1)

        @block.vector
        def _(dve):
            dve.wait_ge(turned, 1)
            nc.vector.tensor_copy(kit.pcol[:, :], pp[:, 0:NCOL]).then_inc(cols_ready, 1)
            nc.vector.tensor_copy(kit.mcol[:, :, :, :, :].rearrange("p a b c k -> p (a b c k)"),
                                  pp[:, 128:192]).then_inc(cols_ready, 1)
            dve.wait_ge(cols_ready, 2)
            for cond in range(2):
                for l in range(DEPTH):
                    nc.vector.scalar_tensor_tensor(kit.scale1[:, cond, l, :], kit.mcol[:, cond, l, 1, :], 1.0,
                                                   kit.pcol[:, COL_N1 + 8 * l:COL_N1 + 8 * l + 8], ALU.add,
                                                   ALU.mult).then_inc(scaled, 1)


def phase_norm_in(kit, layer, sources):
    nc, consts, aT = kit.nc, kit.consts, kit.aT
    with ExitStack() as st:
        sb = lambda n, s, d=F32: st.enter_context(nc.sbuf_tensor(f"ni{layer}_{n}", s, d))
        x, sq, xn = sb("x", [P, 2, D]), sb("sq", [P, 2, D]), sb("xn", [P, 2, D])
        ss, rs = sb("ss", [P, 2]), sb("rs", [P, 2, 2])
        ps = [st.enter_context(nc.psum_tensor(f"ni{layer}_ps{j}", [P, KD, P], F32)) for j in range(2)]
        x_loaded = [kit.sem(f"x_loaded{j}") for j in range(2)]
        x_free, ss_ready, rs_half, rs_ready, xn_ready, turned, act_out, dve_out = (
            kit.sem(n) for n in ("x_free", "ss_ready", "rs_half", "rs_ready", "xn_ready", "turned", "act_out", "dve_out"))
        block = st.enter_context(nc.Block())
        groups, before = [], 0
        for src, tile0, tiles, cond in sources:
            groups.append((src.rearrange("(t p) d -> p t d", p=P), tile0, tiles // 2, cond, before))
            before += tiles

        @block.sync
        def _(sp):
            for src, tile0, pairs, cond, base in groups:
                with sp.Fori(0, pairs) as i:
                    for j in range(2):
                        sp.wait_ge(x_free, i * 2 + (base + j + 1))
                        sp.dma_start(x[:, j, :], src[:, bass.ds(i * 2 + j, 1), :].rearrange("p a d -> p (a d)")).then_inc(x_loaded[j], 16)

        @block.scalar
        def _(act):
            act.sem_inc(x_free, 1)
            act.sem_inc(x_free, 1)
            for src, tile0, pairs, cond, base in groups:
                with act.Fori(0, pairs) as i:
                    for j in range(2):
                        act.wait_ge(x_loaded[j], i * 16 + (base // 2 * 16 + 16))
                        nc.scalar.activation(sq[:, j, :], x[:, j, :], ACT.Square, accum_out=ss[:, j:j + 1]).then_inc(ss_ready, 1)
                    for j in range(2):
                        act.wait_ge(rs_half, i * 4 + (2 * base + 2 * j + 2))
                        nc.scalar.sqrt(rs[:, j, 1:2], rs[:, j, 0:1]).then_inc(rs_ready, 1)
                        act.wait_ge(rs_ready, i * 2 + (base + j + 1))
                        nc.scalar.activation(xn[:, j, :], x[:, j, :], ACT.Copy, scale=rs[:, j, 1:2]).then_inc(xn_ready, 1)
                        act.wait_ge(xn_ready, i * 2 + (base + j + 1))
                        act.sem_inc(x_free, 1)
                    for j in range(2):
                        act.wait_ge(turned, i * 2 + (base + j + 1))
                        for k in range(KD // 2):
                            last = nc.scalar.activation(aT[:, k, bass.ds(i * 256 + (tile0 + j) * P, P)], ps[j][:, k, :], ACT.Identity,
                                                        scale=kit.scale1[:, cond, layer, k:k + 1],
                                                        bias=kit.mcol[:, cond, layer, 0, k:k + 1])
                        last.then_inc(act_out, 1)

        @block.vector
        def _(dve):
            dve.sem_inc(dve_out, 1)
            dve.sem_inc(dve_out, 1)
            for src, tile0, pairs, cond, base in groups:
                with dve.Fori(0, pairs) as i:
                    for j in range(2):
                        dve.wait_ge(ss_ready, i * 2 + (base + j + 1))
                        nc.vector.tensor_scalar(rs[:, j, 0:1], ss[:, j:j + 1], 1.0 / D, EPS, ALU.mult, ALU.add).then_inc(rs_half, 1)
                        dve.wait_ge(rs_half, i * 4 + (2 * base + 2 * j + 1))
                        nc.vector.reciprocal(rs[:, j, 0:1], rs[:, j, 0:1]).then_inc(rs_half, 1)
                    for j in range(2):
                        dve.wait_ge(turned, i * 2 + (base + j + 1))
                        for k in range(KD // 2, KD):
                            last = nc.vector.tensor_scalar(aT[:, k, bass.ds(i * 256 + (tile0 + j) * P, P)], ps[j][:, k, :],
                                                           kit.scale1[:, cond, layer, k:k + 1],
                                                           kit.mcol[:, cond, layer, 0, k:k + 1], ALU.mult, ALU.add)
                        last.then_inc(dve_out, 1)

        @block.tensor
        def _(pe):
            for src, tile0, pairs, cond, base in groups:
                with pe.Fori(0, pairs) as i:
                    for j in range(2):
                        pe.wait_ge(xn_ready, i * 2 + (base + j + 1))
                        pe.wait_ge(dve_out, i * 2 + (base + j + 1))
                        for k in range(KD):
                            last = nc.tensor.transpose(ps[j][:, k, :], xn[:, j, k * P:(k + 1) * P], consts[:, 0:P])
                        last.then_inc(turned, 1)


def host_consts():
    p, f = np.arange(P)[:, None], np.arange(P)[None, :]
    c = np.zeros((P, NCONST), np.float32)
    c[:, C_ID:C_ID + P] = p == f
    c[:, C_GE:C_GE + P] = f >= p
    c[:, C_LE:C_LE + P] = f <= p
    c[:, C_NGE:C_NGE + P] = np.where(f >= p, 0.0, NEG)
    c[:, C_NLE:C_NLE + P] = np.where(f <= p, 0.0, NEG)
    c[:, C_STRICT:C_STRICT + P] = p < f
    c[:, C_ONE:C_ONE + P] = 1.0
    r = np.arange(P)
    c[:, C_FWD] = r < SSD_HEADS
    c[:, C_FWD + 1] = r >= SSD_HEADS
    c[:, C_FWD + 2] = r < ML_HEADS
    c[:, C_FWD + 3] = r >= ML_HEADS
    return c


def phase_in_even(kit):
    nc, A, consts, aT, pcol = kit.nc, kit.A, kit.consts, kit.aT, kit.pcol
    w_in = A["ev_w_in"][0].rearrange("(k p) n -> p k n", p=P)
    HALF = 2 * P
    PAIRS = NCH // 2
    ITER = PAIRS // 2
    ZITER = ZVO // BANK // 2
    TAILW = 72
    TB = ((0, BANK), (BANK, TOK))
    with ExitStack() as st:
        sb = lambda n, s, d=F32: st.enter_context(nc.sbuf_tensor(f"ie_{n}", s, d))
        w_tail = sb("w_tail", [P, KD, TAILW])
        w_conv = [sb(f"w_conv{h}", [P, KD, HALF]) for h in range(2)]
        w_zvo = [sb(f"w_zvo{h}", [P, KD, BANK]) for h in range(2)]
        y = [[sb(f"y{h}{t}", [P, TOK]) for t in range(2)] for h in range(2)]
        feat = [sb(f"feat{h}", [P, 2, TOK]) for h in range(2)]
        tokens = [sb(f"tokens{h}", [P, NT, HALF]) for h in range(2)]
        stage = [sb(f"stage{s}", [P, BANK]) for s in range(4)]
        r = {n: sb(n, [NDT, TOK]) for n in ("x", "e", "ac", "f", "b", "ln", "dt", "da", "keepf", "keepb")}
        r["w"], r["d"], r["m"] = r["ac"], r["f"], r["b"]
        sc = {n: sb("s" + n, [NDT, w]) for n, w in (("bias", 1), ("alog", 1), ("na", 1), ("tot", NT), ("cd", NT))}
        g = {n: sb("g" + n, [NML, TOK]) for n in ("i", "x", "e", "w", "bf", "bb", "ln", "lf", "b", "mm")}
        g["mb"], g["mf"], g["d"], g["m"], g["M"], g["g"] = g["e"], g["w"], g["bf"], g["bb"], g["x"], g["ln"]
        gc = {n: sb("gc" + n, [NML, w]) for n, w in (("ib", 1), ("fb", 1), ("min", NT), ("min2", NT), ("end", NT), ("end2", NT), ("sd", NT))}
        packS, packM = sb("packS", [P, TOK]), sb("packM", [P, TOK])
        pu = [st.enter_context(nc.psum_tensor(f"ie_pu{t}", [P, 2 * BANK], F32)) for t in range(2)]
        px = [st.enter_context(nc.psum_tensor(f"ie_px{t}", [P, NT // 3, 4, P], F32)) for t in range(2)]
        zeros = sb("zeros", [P, D])
        y_rows = kit.y.rearrange("(c p) d -> p c d", p=P)
        SHARE = kit.y.shape[0] // P // (ITER - 1)
        S = lambda n: kit.sem("ie_" + n)
        y_cleared = S("y_cleared")
        tail_clear = S("tail_clear")
        small_loaded, tail_loaded, tail_ready, tail_taken = S("small_loaded"), S("tail_loaded"), S("tail_ready"), S("tail_taken")
        w_loaded = [S(f"w_loaded{h}") for h in range(2)]
        w_free = [S(f"w_free{h}") for h in range(2)]
        z_loaded = [S(f"z_loaded{h}") for h in range(2)]
        u_ready, y_begun, y_ready, u_free, feat_ready = (S(n) for n in ("u_ready", "y_begun", "y_ready", "u_free", "feat_ready"))
        turned, tok_ready, mm_done = S("turned"), S("tok_ready"), S("mm_done")
        feat_stored = [S(f"feat_stored{h}") for h in range(2)]
        tok_stored = [S(f"tok_stored{h}") for h in range(2)]
        z_done = S("z_done")
        turn_done = [S(f"turn_done{h}") for h in range(2)]
        feat_free = [S(f"feat_free{h}") for h in range(2)]
        tok_free = [S(f"tok_free{h}") for h in range(2)]
        stage_free = [S(f"stage_free{s}") for s in range(4)]
        z_taken = [S(f"z_taken{s}") for s in range(4)]
        z_stored = [S(f"z_stored{s}") for s in range(4)]
        chain_v = S("chain_v")
        act_needs, act_gave = S("act_needs"), S("act_gave")
        packs_ready, packs_turned, rows_stored = S("packs_ready"), S("packs_turned"), S("rows_stored")

        def give_back(pool, i, n):
            pool.wait_ge(z_stored[n % 4], i * 48 + n // 4 * 16 + 16)
            pool.sem_inc(stage_free[n % 4], 1)

        def zvo_out(act, start, end):
            with act.Fori(start, end) as i:
                for n in range(2 * NT):
                    s = n % 4
                    act.wait_ge(z_done, i * 2 * NT + n + 1)
                    act.wait_ge(stage_free[s], i * 3 + n // 4 + 1)
                    nc.scalar.copy(stage[s][:, :], pu[s // 2][:, s % 2 * BANK:(s % 2 + 1) * BANK]).then_inc(z_taken[s], 1)

        def gates(dve, V, ch):
            TT, TS, STT, SCAN = V.tensor_tensor, V.tensor_scalar, V.scalar_tensor_tensor, V.tensor_tensor_scan
            fwd32, bwd32 = consts[0:NDT, C_FWD:C_FWD + 1], consts[0:NDT, C_FWD + 1:C_FWD + 2]
            fwd8, bwd8 = consts[0:NML, C_FWD + 2:C_FWD + 3], consts[0:NML, C_FWD + 3:C_FWD + 4]
            A_ = slice(None)

            def pick(dst, f, b, mf, mb):
                ch(TS(dst, f, mf, None, ALU.mult))
                ch(STT(dst, b, mb, dst, ALU.mult, ALU.add))

            def chunks(x):
                return x[:, :].rearrange("r (t q) -> r t q", q=P)

            dve.wait_ge(small_loaded, 64)
            ch(TS(r["x"][:, :], r["x"][:, :], sc["bias"][:, :], None, ALU.add))
            ch(TS(g["i"][:, :], g["i"][:, :], gc["ib"][:, :], None, ALU.add))
            ch(TS(g["x"][:, :], g["x"][:, :], gc["fb"][:, :], None, ALU.add))
            STT(r["e"][:, :], r["x"][:, :], -1.0, r["x"][:, :], ALU.mult, ALU.min)
            STT(g["e"][:, :], g["x"][:, :], -1.0, g["x"][:, :], ALU.mult, ALU.min).then_inc(act_needs, 1)
            dve.wait_ge(act_gave, 3)
            for q in (r, g):
                ch(TS(q["w"][:, :], q["e"][:, :], 1.0, None, ALU.add))
            dve.sem_inc(act_needs, 1)
            for q in (r, g):
                ch(TS(q["d"][:, :], q["w"][:, :], -1.0, None, ALU.add))
                ch(TS(q["m"][:, :], q["d"][:, :], 0.0, None, ALU.is_equal))
                ch(TT(q["d"][:, :], q["d"][:, :], q["m"][:, :], ALU.add))
                ch(V.reciprocal(q["d"][:, :], q["d"][:, :]))
                ch(TT(q["d"][:, :], q["d"][:, :], q["e"][:, :], ALU.mult))
            dve.wait_ge(act_gave, 5)
            for q in (r, g):
                ch(TT(q["ln"][:, :], q["ln"][:, :], q["m"][:, :], ALU.add))
                ch(TT(q["ln"][:, :], q["ln"][:, :], q["d"][:, :], ALU.mult))
            ch(STT(r["dt"][:, :], r["x"][:, :], 0.0, r["ln"][:, :], ALU.max, ALU.add))
            ch(TS(r["da"][:, :], r["dt"][:, :], sc["na"][:, :], -1.0, ALU.mult, ALU.mult))
            ch(STT(g["lf"][:, :], g["x"][:, :], 0.0, g["ln"][:, :], ALU.min, ALU.subtract))
            rev = slice(None, None, -1)
            dve.wait_ge(tail_clear, 3)
            for q, x, f, b, n in ((r, "da", "f", "b", NDT), (g, "lf", "bf", "bb", NML)):
                ch(SCAN(q[f][:, :], r["keepf"][0:n, :], q[x][:, :], 0.0, ALU.mult, ALU.add))
                ch(SCAN(q[b][:, rev], r["keepb"][0:n, rev], q[x][:, rev], 0.0, ALU.mult, ALU.add))
            pick(r["ac"][:, :], r["f"][:, :], r["b"][:, :], fwd32, bwd32)
            pick(sc["tot"][:, :], r["f"][:, P - 1:TOK:P], r["b"][:, 0:TOK:P], fwd32, bwd32)
            pick(g["b"][:, :], g["bf"][:, :], g["bb"][:, :], fwd8, bwd8)
            ch(SCAN(g["mf"][:, :], g["lf"][:, :], g["i"][:, :], 0.0, ALU.add, ALU.max))
            cr = slice(CTX - 1, None, -1)
            lr = slice(TOK - 1, CTX - 1, -1)
            ch(SCAN(g["mb"][:, cr], g["lf"][:, cr], g["i"][:, cr], 0.0, ALU.add, ALU.max))
            ch(SCAN(g["mb"][:, lr], g["lf"][:, lr], g["i"][:, lr], g["mb"][:, 0:1], ALU.add, ALU.max))
            pick(g["mm"][:, :], g["mf"][:, :], g["mb"][:, :], fwd8, bwd8)
            ch(V.memset(gc["min"][:, :], 0.0))
            ch(V.memset(gc["min2"][:, :], 0.0))
            ch(V.tensor_copy(gc["min"][:, 1:NT], g["mf"][:, P - 1:TOK - P:P]))
            ch(V.tensor_copy(gc["min2"][:, 0:1], g["mb"][:, P:P + 1]))
            ch(V.tensor_copy(gc["min2"][:, CT:NT - 1], g["mb"][:, CTX + P:TOK:P]))
            ch(V.tensor_copy(gc["min2"][:, NT - 1:NT], g["mb"][:, 0:1]))
            pick(gc["min"][:, :], gc["min"][:, :], gc["min2"][:, :], fwd8, bwd8)
            ch(TT(g["M"][:, :], g["mm"][:, :], g["b"][:, :], ALU.subtract))
            ch(TT(g["g"][:, :], g["i"][:, :], g["b"][:, :], ALU.subtract))
            pick(gc["end"][:, :], g["M"][:, P - 1:TOK:P], g["M"][:, 0:TOK:P], fwd8, bwd8)
            ch(TT(chunks(r["f"]), sc["tot"][:, :].unsqueeze(2).to_broadcast([NDT, NT, P]), chunks(r["ac"]), ALU.subtract))
            ch(TT(chunks(g["bf"]), gc["min"][:, :].unsqueeze(2).to_broadcast([NML, NT, P]), chunks(g["M"]), ALU.subtract))
            ch(TT(chunks(g["bb"]), chunks(g["g"]), gc["end"][:, :].unsqueeze(2).to_broadcast([NML, NT, P]), ALU.subtract))
            ch(TT(gc["end2"][:, :], gc["min"][:, :], gc["end"][:, :], ALU.subtract))
            dve.sem_inc(act_needs, 1)
            V.tensor_copy(packS[0:NDT, :], r["dt"][:, :])
            V.tensor_copy(packS[32:32 + NDT, :], r["ac"][:, :])
            V.tensor_copy(packM[0:NML, :], g["g"][:, :])
            dve.wait_ge(act_gave, 6)
            V.tensor_tensor(packS[96:96 + NDT, :], r["f"][:, :], r["dt"][:, :], ALU.mult)
            TS(packM[64:64 + NML, :], g["bb"][:, :], float(ML_QK) ** -0.5, None, ALU.mult).then_inc(packs_ready, 1)

        block = st.enter_context(nc.Block())

        @block.sync
        def _(sp):
            small = [(sc["bias"][:, :], A["ev_dt_bias"].rearrange("a d h -> (a d h)")), (sc["alog"][:, :], A["ev_a_log"].rearrange("a d h -> (a d h)")),
                     (gc["ib"][:, :], A["ev_ig_bias"].rearrange("a d h -> (a d h)")), (gc["fb"][:, :], A["ev_fg_bias"].rearrange("a d h -> (a d h)"))]
            sp.wait_ge(tail_clear, 1)
            for at, src, n in ((0, 0, NDT), (32, NDT, NML), (64, NDT + NML, NML)):
                sp.dma_start(w_tail[:, :, at:at + n], w_in[:, :, TAIL0 + src:TAIL0 + src + n]).then_inc(tail_loaded, 16)
            for dst, src in small:
                sp.dma_start(dst, src.rearrange("(n o) -> n o", o=1)).then_inc(small_loaded, 16)
            for h in range(2):
                sp.dma_start(w_conv[h][:, :, :], w_in[:, :, h * HALF:(h + 1) * HALF]).then_inc(w_loaded[h], 16)
            for h in range(2):
                sp.dma_start(w_zvo[h][:, :, :], w_in[:, :, CONV_CH + h * BANK:CONV_CH + (h + 1) * BANK]).then_inc(z_loaded[h], 16)
            sp.wait_ge(tail_clear, 1)
            with sp.Fori(1, ITER) as i:
                for h in range(2):
                    sp.wait_ge(w_free[h], i)
                    sp.dma_start(w_conv[h][:, :, :], w_in[:, :, bass.ds(i * 2 * HALF + h * HALF, HALF)]).then_inc(w_loaded[h], 16)
                sp.dma_start(y_rows[:, bass.ds((i - 1) * SHARE, SHARE), :], zeros[:, :].unsqueeze(1).to_broadcast([P, SHARE, D])).then_inc(y_cleared, 16)
            with sp.Fori(1, ZITER) as i:
                for h in range(2):
                    sp.wait_ge(z_done, (i - 1) * 2 * NT + (h + 1) * NT)
                    sp.dma_start(w_zvo[h][:, :, :], w_in[:, :, bass.ds(i * 2 * BANK + (CONV_CH + h * BANK), BANK)]).then_inc(z_loaded[h], 16)
            sp.wait_ge(packs_ready, 1)
            for dst, src in ((kit.ac_rows, r["ac"][:, :]), (kit.M_rows, g["M"][:, :]), (kit.cd_rows, sc["cd"][:, :]), (kit.sd_rows, gc["sd"][:, :])):
                sp.dma_start(dst, src).then_inc(rows_stored, 16)
            sp.wait_ge(y_cleared, 16 * (ITER - 1))
            sp.wait_ge(rows_stored, 64)

        @block.tensor
        def _(pe):
            pe.wait_ge(tail_loaded, 48)
            for n, (a, b) in enumerate(TB):
                for k in range(KD):
                    last = nc.tensor.matmul(pu[0][0:TAILW, a:b], w_tail[:, k, :], aT[:, k, a:b], start=(k == 0), stop=(k == KD - 1))
            last.then_inc(tail_ready, 1)
            pe.wait_ge(tail_taken, 1)

            def project(i, h, tile0):
                pe.wait_ge(w_loaded[h], i * 16 + 16)
                for t in range(2):
                    pe.wait_ge(u_free, tile0 + t + 1)
                    for a, b in TB:
                        for k in range(KD):
                            last = nc.tensor.matmul(pu[t][:, a:b], w_conv[h][:, k, t * P:(t + 1) * P], aT[:, k, a:b],
                                                    start=(k == 0), stop=(k == KD - 1))
                    last.then_inc(u_ready, 1)
                    if t == 1:
                        pe.wait_ge(u_ready, tile0 + 2)
                        pe.sem_inc(w_free[h], 1)

            def turn(h, tile0):
                for t in range(2):
                    pe.wait_ge(feat_ready, tile0 + t + 1)
                    pe.wait_ge(tok_ready, tile0 + t + 1)
                    for T in range(NT):
                        last = nc.tensor.transpose(px[t][:, T // 4, T % 4, :], feat[h][:, t, T * P:(T + 1) * P], consts[:, 0:P])
                    last.then_inc(turned, 1)
                pe.wait_ge(turned, tile0 + 2)
                pe.sem_inc(turn_done[h], 1)

            for h in range(2):
                pe.sem_inc(turn_done[h], 1)
            project(0, 0, 0)
            project(0, 1, 2)
            turn(0, 0)
            with pe.Fori(1, ITER) as i:
                project(i, 0, i * 4)
                turn(1, i * 4 - 2)
                project(i, 1, i * 4 + 2)
                turn(0, i * 4)
            turn(1, NCH - 2)
            pe.wait_ge(u_free, NCH + 2)
            with pe.Fori(0, ZITER) as i:
                for h in range(2):
                    pe.wait_ge(z_loaded[h], i * 16 + 16)
                    for T in range(NT):
                        n = h * NT + T
                        bank = n % 4
                        pe.wait_ge(z_taken[bank], i * 3 + n // 4 + 1)
                        for k in range(KD):
                            last = nc.tensor.matmul(pu[bank // 2][:, bank % 2 * BANK:(bank % 2 + 1) * BANK], aT[:, k, T * P:(T + 1) * P],
                                                    w_zvo[h][:, k, :], start=(k == 0), stop=(k == KD - 1))
                        last.then_inc(z_done, 1)
            pe.wait_ge(packs_ready, 1)
            pe.wait_ge(tok_ready, NCH + 2)
            for T in range(NT):
                nc.tensor.transpose(px[0][:, T // 4, T % 4, :], packS[:, T * P:(T + 1) * P], consts[:, 0:P])
            for T in range(NT):
                last = nc.tensor.transpose(px[1][:, T // 4, T % 4, :], packM[:, T * P:(T + 1) * P], consts[:, 0:P])
            last.then_inc(packs_turned, 1)

        @block.gpsimd
        def _(pool):
            nc.gpsimd.memset(zeros[:, :], 0.0)
            nc.gpsimd.memset(w_tail[:, :, :], 0.0).then_inc(tail_clear, 1)
            nc.gpsimd.memset(packM[:, :], 0.0)
            for keep in (r["keepf"], r["keepb"]):
                last = nc.gpsimd.memset(keep[:, :], 1.0)
            last.then_inc(tail_clear, 1)
            pool.wait_ge(tail_clear, 2)
            nc.gpsimd.memset(r["keepf"][:, 0:TOK:P], 0.0)
            nc.gpsimd.memset(r["keepb"][:, P - 1:TOK:P], 0.0).then_inc(tail_clear, 1)
            for h in range(2):
                pool.sem_inc(feat_free[h], 1)
                pool.sem_inc(tok_free[h], 1)

            def store_tokens(c, h, n):
                pool.wait_ge(tok_ready, c + 4)
                pool.dma_start(kit.tokc.rearrange("(T p) n -> p T n", p=P)[:, :, bass.ds(c * P, HALF)], tokens[h][:, :, :]).then_inc(tok_stored[h], 16)
                pool.wait_ge(tok_stored[h], n * 16)
                pool.sem_inc(tok_free[h], 1)

            def store_feat(c, h, n):
                pool.wait_ge(feat_ready, c + 2)
                pool.dma_start(kit.feat[bass.ds(c, 2), :, :].rearrange("c p t -> p c t"), feat[h][:, :, :]).then_inc(feat_stored[h], 16)
                pool.wait_ge(feat_stored[h], n * 16)
                pool.sem_inc(feat_free[h], 1)

            store_feat(0, 0, 1)
            store_feat(2, 1, 1)
            store_tokens(0, 0, 1)
            with pool.Fori(1, ITER) as i:
                store_feat(i * 4, 0, i + 1)
                store_tokens(i * 4 - 2, 1, i)
                store_feat(i * 4 + 2, 1, i + 1)
                store_tokens(i * 4, 0, i + 1)
            store_tokens(NCH - 2, 1, ITER)
            for s in range(4):
                pool.sem_inc(stage_free[s], 1)
            with pool.Fori(0, ZITER) as i:
                for h in range(2):
                    for T in range(NT):
                        n = h * NT + T
                        s = n % 4
                        pool.wait_ge(z_taken[s], i * 3 + n // 4 + 2)
                        pool.dma_start(kit.zvo[T * P:(T + 1) * P, bass.ds(i * 2 * BANK + h * BANK, BANK)], stage[s][:, :]).then_inc(z_stored[s], 16)
                        if n >= 2:
                            give_back(pool, i, n - 2)
                for n in (2 * NT - 2, 2 * NT - 1):
                    give_back(pool, i, n)

        @block.scalar
        def _(act):
            with act.Fori(0, ITER) as i:
                for h in range(2):
                    for t in range(2):
                        c = i * 4 + 2 * h + t
                        act.wait_ge(u_ready, c + 1)
                        nc.scalar.activation(y[h][t][:, :], pu[t][:, 0:TOK], ACT.Identity, scale=pcol[:, bass.ds(c + (COL_W + NCH), 1)],
                                             bias=pcol[:, bass.ds(c + COL_B, 1)]).then_inc(y_begun, 1)
                    act.wait_ge(feat_free[h], i + 1)
                    act.wait_ge(turn_done[h], i + 1)
                    for t in range(2):
                        c = i * 4 + 2 * h + t
                        act.wait_ge(y_ready, c + 1)
                        nc.scalar.activation(feat[h][:, t, :], y[h][t][:, :], ACT.Silu).then_inc(feat_ready, 1)
                    act.wait_ge(feat_ready, i * 4 + 2 * h + 2)
            for n, (dst, src, func, scale) in enumerate(((r["e"], r["e"], ACT.Exp, 1.0), (g["e"], g["e"], ACT.Exp, 1.0), (sc["na"], sc["alog"], ACT.Exp, 1.0),
                                                         (r["ln"], r["w"], ACT.Ln, 1.0), (g["ln"], g["w"], ACT.Ln, 1.0))):
                act.wait_ge(act_needs, 1 if n < 3 else 2)
                nc.scalar.activation(dst[:, :], src[:, :], func, scale=scale).then_inc(act_gave, 1)
            for s in range(4):
                act.sem_inc(z_taken[s], 1)
            zvo_out(act, 0, 1)
            act.wait_ge(act_needs, 3)
            nc.scalar.activation(packS[64:96, :], r["ac"][:, :], ACT.Exp)
            nc.scalar.activation(r["f"][:, :], r["f"][:, :], ACT.Exp)
            nc.scalar.activation(sc["cd"][:, :], sc["tot"][:, :], ACT.Exp)
            nc.scalar.activation(packM[32:40, :], g["bf"][:, :], ACT.Exp)
            nc.scalar.activation(g["bb"][:, :], g["bb"][:, :], ACT.Exp)
            nc.scalar.activation(packM[96:104, :], g["mm"][:, :], ACT.Exp, scale=-1.0)
            nc.scalar.activation(gc["sd"][:, :], gc["end2"][:, :], ACT.Exp).then_inc(act_gave, 1)
            zvo_out(act, 1, ZITER)
            act.wait_ge(packs_turned, 1)
            nc.scalar.copy(kit.tokM[:, :, :].rearrange("p t c -> p (t c)"), px[1][:, :, :, :].rearrange("p a b c -> p (a b c)")[:, 0:NT * P])

        @block.vector
        def _(dve):
            V = nc.vector
            ch = Chain(dve, chain_v)
            for _n in range(2):
                dve.sem_inc(u_free, 1)
                dve.sem_inc(tok_ready, 1)
            dve.wait_ge(tail_ready, 1)
            V.tensor_copy(r["x"][:, :], pu[0][0:NDT, 0:TOK])
            V.tensor_copy(g["i"][:, :], pu[0][32:32 + NML, 0:TOK])
            V.tensor_copy(g["x"][:, :], pu[0][64:64 + NML, 0:TOK]).then_inc(tail_taken, 1)

            def taps(c0, h):
                for t in range(2):
                    c = c0 + t
                    dve.wait_ge(y_begun, c + 1)
                    for n, tap in enumerate((0, 2)):
                        for a, b in ((0, CTX), (CTX, TOK)):
                            o, u = (slice(a + 1, b), slice(a, b - 1)) if tap == 0 else (slice(a, b - 1), slice(a + 1, b))
                            last = V.scalar_tensor_tensor(y[h][t][:, o], pu[t][:, u], pcol[:, bass.ds(c + (COL_W + tap * NCH), 1)],
                                                          y[h][t][:, o], ALU.mult, ALU.add)
                            if n == 0:
                                ch(last)
                    last.then_inc(y_ready, 1)
                    dve.wait_ge(y_ready, c + 1)
                    dve.sem_inc(u_free, 1)

            def to_tokens(c0, h, n):
                dve.wait_ge(tok_free[h], n)
                for t in range(2):
                    dve.wait_ge(turned, c0 + t + 1)
                    V.tensor_copy(tokens[h][:, :, t * P:(t + 1) * P],
                                  px[t][:, :, :, :].rearrange("p a b c -> p (a b) c")[:, 0:NT, :]).then_inc(tok_ready, 1)

            taps(0, 0)
            taps(2, 1)
            to_tokens(0, 0, 1)
            with dve.Fori(1, ITER) as i:
                ch.enter(i - 1, 8)
                taps(i * 4, 0)
                to_tokens(i * 4 - 2, 1, i)
                taps(i * 4 + 2, 1)
                to_tokens(i * 4, 0, i + 1)
                ch.leave(ITER - 1)
            to_tokens(NCH - 2, 1, ITER)
            gates(dve, V, ch)
            dve.wait_ge(packs_turned, 1)
            V.tensor_copy(kit.tokS[:, :, :].rearrange("p t c -> p (t c)"), px[0][:, :, :, :].rearrange("p a b c -> p (a b c)")[:, 0:NT * P])


def phase_recurrent(kit):
    nc, consts = kit.nc, kit.consts
    HD, MV = SSD_HEADS * SSD_P, ML_HEADS * ML_V
    NV1 = ML_V + 1
    feat_v = kit.feat[8:NCH, :, :].rearrange("c p t -> p c t")
    with ExitStack() as st:
        sb = lambda n, s, d=F32: st.enter_context(nc.sbuf_tensor(f"rc_{n}", s, d))
        two = lambda n, s: [sb(f"{n}{d}", s) for d in range(2)]
        ps = lambda n, s: st.enter_context(nc.psum_tensor(f"rc_{n}", s, F32))
        bcq = two("bcq", [P, 12, P])
        xb = two("xb", [P, HD + SSD_GROUPS * SSD_STATE])
        kt = two("kt", [P, ML_HEADS, ML_QK])
        v1 = two("v1", [P, ML_HEADS, NV1])
        mt = two("mt", [P, SSD_HEADS, P])
        pt = two("pt", [P, ML_HEADS, P])
        colS, colM, colN = two("colS", [P, P]), two("colM", [P, P]), two("colN", [P, ML_HEADS])
        xdt, xde, kw = two("xdt", [P, SSD_HEADS, SSD_P]), two("xde", [P, SSD_HEADS, SSD_P]), two("kw", [P, ML_HEADS, ML_QK])
        cbm, qkm = two("cbm", [P, SSD_GROUPS, P]), two("qkm", [P, ML_HEADS, P])
        yo, ho, inter = two("yo", [P, SSD_HEADS, SSD_P]), two("ho", [P, ML_HEADS, ML_V]), two("inter", [P, ML_HEADS, ML_V])
        hst, hcd = two("hst", [P, SSD_HEADS, SSD_P]), sb("hcd", [P, SSD_HEADS, SSD_P])
        cst = two("cst", [P, ML_HEADS, NV1])
        cdb, sdb, sdc = sb("cdb", [P, NDT, NT]), sb("sdb", [P, NML, NT]), sb("sdc", [P, ML_HEADS])
        den = sb("den", [P, 2, ML_HEADS])
        ps_cb, ps_qk = ps("ps_cb", [P, BANK]), ps("ps_qk", [P, BANK])
        ps_y, ps_o, ps_n = ps("ps_y", [P, HD]), ps("ps_o", [P, HD]), ps("ps_n", [P, MV])
        S = lambda n: kit.sem("rc_" + n)
        passed = S("passed")
        loaded, slot_free = [S(f"loaded{d}") for d in range(2)], [S(f"slot_free{d}") for d in range(2)]
        decays_loaded, begun, cols_ready, x_ready, kw_ready, hcd_ready, added = (
            S(n) for n in ("decays_loaded", "begun", "cols_ready", "x_ready", "kw_ready", "hcd_ready", "added"))
        nv_ready, relu_done = S("nv_ready"), S("relu_done")
        exp_ready, pexp_ready, inter_ready = S("exp_ready"), S("pexp_ready"), S("inter_ready")
        scores_ready, yoff_ready, qc_ready, ydiag_ready, num_ready, hloc_ready, cloc_ready, step_done = (
            S(n) for n in ("scores_ready", "yoff_ready", "qc_ready", "ydiag_ready", "num_ready", "hloc_ready", "cloc_ready", "step_done"))
        scores_taken, mt_ready, pt_ready, yoff_taken, yo_ready, num_taken, ho_ready, h_ready, c_ready = (
            S(n) for n in ("scores_taken", "mt_ready", "pt_ready", "yoff_taken", "yo_ready", "num_taken", "ho_ready", "h_ready", "c_ready"))
        chain_v, sums_cleared = S("chain_v"), S("sums_cleared")
        block = st.enter_context(nc.Block())
        SEGMENTS = ((0, CT, CT - 1), (CT, NT, NT + CT - 1))

        def spare(turn):
            return 1 if turn == SEGMENTS[0][2] else 2

        def steps(eng, body):
            for start, end, turn in SEGMENTS:
                with eng.Fori(start, end) as i:
                    for d in range(2):
                        body(i, d, i if d == 0 else turn - i, turn)

        @block.sync
        def _(sp):
            sp.dma_start(cdb[:, :, :], kit.cd_rows.partition_broadcast(P)).then_inc(decays_loaded, 16)
            sp.dma_start(sdb[:, :, :], kit.sd_rows.partition_broadcast(P)).then_inc(decays_loaded, 16)

            def load(i, d, T, turn):
                wait_alone(sp, slot_free[d], i + 1, passed)
                rows = bass.ds(T * P, P)
                for dst, src in ((mt[d][:, :, :], kit.ac_rows[16 * d:16 * d + 16, rows].partition_broadcast(P)),
                                 (pt[d][:, :, :], kit.M_rows[4 * d:4 * d + 4, rows].partition_broadcast(P)),
                                 (xb[d][:, :], kit.tokc[rows, 0:HD + 256]),
                                 (bcq[d][:, :, :], feat_v[:, :, rows]),
                                 (kt[d][:, :, :].rearrange("p h k -> p (h k)"), kit.tokc[rows, 2048:CONV_CH]),
                                 (v1[d][:, :, 0:ML_V], kit.zvo[rows, D:2 * D].rearrange("p (h v) -> p h v", v=ML_V))):
                    sp.dma_start(dst, src).then_inc(loaded[d], 16)

            steps(sp, load)

        @block.gpsimd
        def _(pool):
            G = nc.gpsimd
            for d in range(2):
                G.memset(v1[d][:, :, ML_V:NV1], 1.0)
                G.memset(hst[d][:, :, :], 0.0)
                last = G.memset(cst[d][:, :, :], 0.0)
            last.then_inc(begun, 1)
            pool.wait_ge(begun, 1)
            pool.sem_inc(added, 1)
            pool.wait_ge(decays_loaded, 32)

            def add_up(n, d, T, count):
                wait_alone(pool, yo_ready, n + 1, passed)
                G.tensor_tensor(kit.yacc[:, bass.ds(T, 1), :].rearrange("p a x -> p (a x)"), kit.yacc[:, bass.ds(T, 1), :].rearrange("p a x -> p (a x)"),
                                yo[d][:, :, :].rearrange("p h x -> p (h x)"), ALU.add)
                pool.wait_ge(ho_ready, n + 1)
                G.tensor_tensor(kit.hacc[:, bass.ds(T, 1), :].rearrange("p a x -> p (a x)"), kit.hacc[:, bass.ds(T, 1), :].rearrange("p a x -> p (a x)"),
                                ho[d][:, :, :].rearrange("p h x -> p (h x)"), ALU.add).then_inc(added, 1)
                wait_alone(pool, added, count, passed)

            def step(i, d, T, turn):
                n = i * 2 + d
                wait_alone(pool, loaded[d], i * 96 + 96, passed)
                wait_alone(pool, cols_ready, n + 1, passed)
                xs = xb[d][:, 0:HD].rearrange("p (h x) -> p h x", x=SSD_P)
                for dst, c in ((xdt, 0), (xde, 96)):
                    cols = colS[d][:, c + 16 * d:c + 16 * d + 16].unsqueeze(2).to_broadcast([P, SSD_HEADS, SSD_P])
                    last = G.tensor_tensor(dst[d][:, :, :], xs, cols, ALU.mult)
                last.then_inc(x_ready, 1)
                G.tensor_tensor(kw[d][:, :, :], kt[d][:, :, :], colM[d][:, 64 + 4 * d:68 + 4 * d].unsqueeze(2).to_broadcast([P, ML_HEADS, ML_QK]),
                                ALU.mult).then_inc(kw_ready, 1)
                if d == 0:
                    add_up(n, 1, turn + 1 - i, n + spare(turn) + 1)
                else:
                    add_up(n, 0, i, n + spare(turn) + 1)
                wait_alone(pool, h_ready, n + 1, passed)
                G.tensor_tensor(hcd[:, :, :], hst[d][:, :, :], cdb[:, 16 * d:16 * d + 16, bass.ds(T, 1)].to_broadcast([P, SSD_HEADS, SSD_P]),
                                ALU.mult).then_inc(hcd_ready, 1)

            for start, end, turn in SEGMENTS:
                with pool.Fori(start, end) as i:
                    for d in range(2):
                        step(i, d, i if d == 0 else turn - i, turn)
                add_up(2 * end, 1, turn + 1 - end, 2 * end + spare(turn) + 1)

        @block.scalar
        def _(act):
            def step(i, d, T, turn):
                n = i * 2 + d
                act.wait_ge(loaded[d], i * 96 + 96)
                nc.scalar.copy(colS[d][:, :], kit.tokS[:, bass.ds(T, 1), :].rearrange("p a c -> p (a c)"))
                nc.scalar.activation(colN[d][:, :], kit.tokM[:, bass.ds(T, 1), 4 * d:4 * d + 4].rearrange("p a c -> p (a c)"), ACT.Copy, scale=-1.0)
                nc.scalar.copy(colM[d][:, :], kit.tokM[:, bass.ds(T, 1), :].rearrange("p a c -> p (a c)")).then_inc(cols_ready, 1)
                act.wait_ge(cols_ready, n + 1)
                for h in range(SSD_HEADS):
                    last = nc.scalar.activation(mt[d][:, h, :], mt[d][:, h, :], ACT.Relu, scale=-1.0, bias=colS[d][:, 32 + 16 * d + h:33 + 16 * d + h])
                last.then_inc(relu_done, 1)
                for h in range(ML_HEADS):
                    last = nc.scalar.activation(pt[d][:, h, :], pt[d][:, h, :], ACT.Relu, bias=colN[d][:, h:h + 1])
                last.then_inc(relu_done, 1)
                act.wait_ge(relu_done, n * 2 + 1)
                nc.scalar.activation(mt[d][:, :, :], mt[d][:, :, :], ACT.Exp, scale=-1.0).then_inc(exp_ready, 1)
                act.wait_ge(relu_done, n * 2 + 2)
                nc.scalar.activation(pt[d][:, :, :], pt[d][:, :, :], ACT.Exp, scale=-1.0).then_inc(pexp_ready, 1)
                act.wait_ge(qc_ready, n + 1)
                act.wait_ge(num_taken, n + 1)
                for h in range(ML_HEADS):
                    last = nc.scalar.activation(inter[d][:, h, :], ps_n[:, h * ML_V:(h + 1) * ML_V], ACT.Copy,
                                                scale=colM[d][:, 32 + 4 * d + h:33 + 4 * d + h])
                last.then_inc(inter_ready, 1)

            steps(act, step)

        @block.tensor
        def _(pe):
            MM = nc.tensor.matmul
            pe.wait_ge(begun, 1)

            def step(i, d, T, turn):
                n = i * 2 + d
                pe.wait_ge(loaded[d], i * 96 + 96)
                pe.wait_ge(nv_ready, n + 1)
                for g in range(SSD_GROUPS):
                    MM(ps_cb[:, g * P:(g + 1) * P], bcq[d][:, g, :], bcq[d][:, 2 + g, :], start=True, stop=True)
                for h in range(ML_HEADS):
                    last = MM(ps_qk[:, h * P:(h + 1) * P], bcq[d][:, 8 + h, :], bcq[d][:, 4 + h, :], start=True, stop=True)
                last.then_inc(scores_ready, 1)
                pe.wait_ge(h_ready, n + 1)
                for g in range(SSD_GROUPS):
                    last = MM(ps_o[:, g * BANK:(g + 1) * BANK], bcq[d][:, 2 + g, :], hst[d][:, g * 8:g * 8 + 8, :], start=True, stop=True)
                last.then_inc(yoff_ready, 1)
                for h in range(ML_HEADS):
                    last = MM(ps_n[:, h * ML_V:(h + 1) * ML_V], bcq[d][:, 4 + h, :], cst[d][:, h, 0:ML_V], start=True, stop=True)
                last.then_inc(qc_ready, 1)
                pe.wait_ge(c_ready, n + 1)
                pe.wait_ge(mt_ready, n + 1)
                pe.wait_ge(x_ready, n + 1)
                for h in range(SSD_HEADS):
                    last = MM(ps_y[:, h * SSD_P:(h + 1) * SSD_P], mt[d][:, h, :], xdt[d][:, h, :], start=True, stop=True)
                last.then_inc(ydiag_ready, 1)
                pe.wait_ge(pt_ready, n + 1)
                pe.wait_ge(inter_ready, n + 1)
                for h in range(ML_HEADS):
                    MM(ps_n[:, h * ML_V:(h + 1) * ML_V], pt[d][:, h, :], v1[d][:, h, 0:ML_V], start=True, stop=True)
                for h in range(ML_HEADS):
                    MM(ps_cb[:, h:h + 1], bcq[d][:, 4 + h, :], cst[d][:, h, ML_V:NV1], start=True, stop=True)
                    last = MM(ps_cb[:, 4 + h:5 + h], pt[d][:, h, :], v1[d][:, h, ML_V:NV1], start=True, stop=True)
                last.then_inc(num_ready, 1)
                pe.wait_ge(yoff_taken, n + 1)
                for g in range(SSD_GROUPS):
                    last = MM(ps_o[:, g * BANK:(g + 1) * BANK], xb[d][:, HD + g * P:HD + (g + 1) * P], xde[d][:, g * 8:g * 8 + 8, :], start=True, stop=True)
                last.then_inc(hloc_ready, 1)
                pe.wait_ge(kw_ready, n + 1)
                pe.wait_ge(yo_ready, n + 2)
                for h in range(ML_HEADS):
                    MM(ps_y[:, h * ML_V:(h + 1) * ML_V], kw[d][:, h, :], v1[d][:, h, 0:ML_V], start=True, stop=True)
                for h in range(ML_HEADS):
                    last = MM(ps_qk[:, h:h + 1], kw[d][:, h, :], v1[d][:, h, ML_V:NV1], start=True, stop=True)
                last.then_inc(cloc_ready, 1)

            steps(pe, step)

        @block.vector
        def _(dve):
            V = nc.vector
            TT, STT = V.tensor_tensor, V.scalar_tensor_tensor
            ch = Chain(dve, chain_v)
            for d in range(2):
                V.memset(yo[d][:, :, :], 0.0)
                V.memset(ho[d][:, :, :], 0.0)
            V.memset(kit.yacc[:, :, :], 0.0)
            V.memset(kit.hacc[:, :, :], 0.0).then_inc(sums_cleared, 1)
            for d in range(2):
                dve.sem_inc(slot_free[d], 1)
            dve.wait_ge(sums_cleared, 1)
            dve.wait_ge(begun, 1)
            dve.wait_ge(decays_loaded, 32)
            for s, k in ((c_ready, 1), (nv_ready, 1), (yo_ready, 1), (ho_ready, 1), (h_ready, 1), (num_taken, 2)):
                for _n in range(k):
                    dve.sem_inc(s, 1)
            LINKS = 10

            def step(i, d, T, turn):
                n = i * 2 + d
                wait_alone(dve, loaded[d], i * 96 + 96, passed)
                ch(V.tensor_copy(sdc[:, :], sdb[:, 4 * d:4 * d + 4, bass.ds(T, 1)].rearrange("p h a -> p (h a)")))
                mask = consts[:, C_GE:C_GE + P] if d == 0 else consts[:, C_LE:C_LE + P]
                dve.wait_ge(scores_ready, n + 1)
                ch(TT(cbm[d][:, :, :], ps_cb[:, 0:SSD_GROUPS * P].rearrange("p (g l) -> p g l", l=P), mask.unsqueeze(1).to_broadcast([P, SSD_GROUPS, P]), ALU.mult))
                ch(STT(qkm[d][:, :, :], ps_qk[:, :].rearrange("p (h l) -> p h l", l=P), float(ML_QK) ** -0.5,
                       mask.unsqueeze(1).to_broadcast([P, ML_HEADS, P]), ALU.mult, ALU.mult))
                dve.wait_ge(exp_ready, n + 1)
                four = mt[d][:, :, :].rearrange("p (g r) l -> p g r l", g=SSD_GROUPS)
                TT(four, four, cbm[d][:, :, :].unsqueeze(2).to_broadcast([P, SSD_GROUPS, 8, P]), ALU.mult).then_inc(mt_ready, 1)
                dve.wait_ge(pexp_ready, n + 1)
                TT(pt[d][:, :, :], pt[d][:, :, :], qkm[d][:, :, :], ALU.mult).then_inc(pt_ready, 1)
                dve.wait_ge(yoff_ready, n + 1)
                dve.wait_ge(added, n + spare(turn))
                TT(yo[d][:, :, :], ps_o[:, :].rearrange("p (h x) -> p h x", x=SSD_P),
                   colS[d][:, 64 + 16 * d:80 + 16 * d].unsqueeze(2).to_broadcast([P, SSD_HEADS, SSD_P]), ALU.mult).then_inc(yoff_taken, 1)
                dve.wait_ge(yoff_taken, n + 1)
                dve.wait_ge(ydiag_ready, n + 1)
                TT(yo[d][:, :, :], yo[d][:, :, :], ps_y[:, :].rearrange("p (h x) -> p h x", x=SSD_P), ALU.add).then_inc(yo_ready, 1)
                dve.wait_ge(num_ready, n + 1)
                ch(TT(den[:, 0, :], ps_cb[:, 0:4], colM[d][:, 32 + 4 * d:36 + 4 * d], ALU.mult))
                ch(TT(den[:, 0, :], den[:, 0, :], ps_cb[:, 4:8], ALU.add))
                ch(STT(den[:, 1, :], den[:, 0, :], -1.0, den[:, 0, :], ALU.mult, ALU.max))
                ch(TT(den[:, 1, :], den[:, 1, :], colM[d][:, 96 + 4 * d:100 + 4 * d], ALU.max))
                ch(V.reciprocal(den[:, 0, :], den[:, 1, :]))
                ch(TT(ho[d][:, :, :], ps_n[:, :].rearrange("p (h x) -> p h x", x=ML_V), inter[d][:, :, :], ALU.add))
                dve.sem_inc(num_taken, 1)
                TT(ho[d][:, :, :], ho[d][:, :, :], den[:, 0, :].unsqueeze(2).to_broadcast([P, ML_HEADS, ML_V]), ALU.mult).then_inc(ho_ready, 1)
                dve.wait_ge(hloc_ready, n + 1)
                dve.wait_ge(hcd_ready, n + 1)
                TT(hst[d][:, :, :], hcd[:, :, :], ps_o[:, :].rearrange("p (h x) -> p h x", x=SSD_P), ALU.add).then_inc(h_ready, 1)
                dve.wait_ge(cloc_ready, n + 1)
                nv = cst[d][:, :, ML_V:NV1].rearrange("p h a -> p (h a)")
                ch(TT(nv, nv, sdc[:, :], ALU.mult))
                TT(nv, nv, ps_qk[:, 0:4], ALU.add).then_inc(nv_ready, 1)
                for h in range(ML_HEADS):
                    last = STT(cst[d][:, h, 0:ML_V], cst[d][:, h, 0:ML_V], sdc[:, h:h + 1], ps_y[:, h * ML_V:(h + 1) * ML_V], ALU.mult, ALU.add)
                last.then_inc(c_ready, 1)
                dve.wait_ge(c_ready, n + 2)
                dve.sem_inc(slot_free[d], 1)

            for start, end, turn in SEGMENTS:
                with dve.Fori(start, end) as i:
                    ch.enter(i - start, 2 * LINKS)
                    for d in range(2):
                        step(i, d, i if d == 0 else turn - i, turn)
                    ch.leave(end - start)


def phase_out(kit, layer, sources, w_out, K, h_out):
    nc, A, consts = kit.nc, kit.A, kit.consts
    even = layer == 0
    NG_S, NG_M = SSD_GROUPS, ML_HEADS
    W_S, W_M = D // NG_S, D // NG_M
    base_mod = layer * 6 * D
    with ExitStack() as st:
        sb = lambda n, s, d=F32: st.enter_context(nc.sbuf_tensor(f"po{layer}_{n}", s, d))
        ps = lambda n, s: st.enter_context(nc.psum_tensor(f"po{layer}_{n}", s, F32))
        w = sb("w", [P, K, D])
        gate, sc2, sh2 = ([sb(f"{n}{s}", [P, D]) for s in range(len(sources))] for n in ("gate", "sc2", "sh2"))
        w2 = sb("w2", [P, D])
        h = [sb(f"h{j}", [P, D]) for j in range(2)]
        yT, n1, mix = sb("yT", [P, 2 * KD, P]), sb("n1", [P, D]), sb("mix", [P, K * P])
        junk = sb("junk", [P, D])
        ss, rs = sb("ss", [P, 8]), sb("rs", [P, 8])
        s2, r2 = sb("s2", [P, 2]), sb("r2", [P, 2])
        tT = yT
        wr = sb("wr", [P, KD, 20])
        if even:
            xs, zo, dsk = sb("xs", [P, D]), sb("zo", [P, 2, D]), sb("dsk", [P, SSD_HEADS])
        ps_t = ps("ps_t", [P, 2 * KD, P])
        ps_y = ps("ps_y", [P, D])
        ps_r = ps("ps_r", [P, BANK])
        S = lambda n: kit.sem(f"po{layer}_" + n)
        passed = S("passed")
        w_loaded, skip_loaded, rows_loaded, w_ready, s2_ready = [S(f"w_loaded{c}") for c in range(2)], S("skip_loaded"), S("rows_loaded"), S("w_ready"), S("s2_ready")
        in_loaded, in_free, h_loaded, h_free = S("in_loaded"), S("in_free"), [S(f"h_loaded{j}") for j in range(2)], [S(f"h_free{j}") for j in range(2)]
        skip_ready, gates_ready, yg_ready, ss_ready, rs_half, rs_ready, mix_ready = (
            S(n) for n in ("skip_ready", "gates_ready", "yg_ready", "ss_ready", "rs_half", "rs_ready", "mix_ready"))
        turned, yT_act, yT_dve, y_ready, gated, h_ready, sq_ready, r2_half, r2_ready, n_ready, tm_ready, t_ready = (
            S(n) for n in ("turned", "yT_act", "yT_dve", "y_ready", "gated", "h_ready", "sq_ready", "r2_half", "r2_ready", "n_ready", "tm_ready", "t_ready"))
        h_stored, t_stored = [S(f"h_stored{j}") for j in range(2)], S("t_stored")
        t_turned, tT_ready, logits_done, logits_out = S("t_turned"), S("tT_ready"), S("logits_done"), S("logits_out")
        junked, h_junked, y_taken, mix_free, chain_v = S("junked"), S("h_junked"), S("y_taken"), S("mix_free"), S("chain_v")
        JUNKS = NG_S + NG_M
        ROWS = 16 * (1 + 3 * len(sources) + 2)
        block = st.enter_context(nc.Block())
        src_y = kit.yacc
        first = sources[0][1]
        groups, before = [], 0
        for s, (src, tile0, tiles, cond) in enumerate(sources):
            groups.append((src.rearrange("(t p) d -> p t d", p=P), tile0, tiles // 2, cond, s, before))
            before += tiles
        count = before

        def tiles_of(eng, body, chain=None, links=0):
            for g, (src, tile0, pairs, cond, s, base) in enumerate(groups):
                last = g == len(groups) - 1
                looped = pairs - 1 if last else pairs
                if looped:
                    with eng.Fori(0, looped) as i:
                        if chain:
                            chain.enter(i, 2 * links)
                        for j in range(2):
                            body(i * 2 + (tile0 + j), i * 2 + (base + j), i + base // 2, j, src, i * 2 + j, s, True)
                        if chain:
                            chain.leave(looped)
                if last:
                    for j in range(2):
                        t = looped * 2 + j
                        body(tile0 + t, base + t, (base + t) // 2, j, src, t, s, j == 0)

        @block.sync
        def _(sp):
            if even:
                sp.dma_start(dsk[:, :], A["ev_d_skip"][0].partition_broadcast(P)).then_inc(skip_loaded, 16)

            def load(T, n, m, j, src, t, s, more):
                rows_T = bass.ds(T * P, P)
                if even:
                    sp.wait_ge(in_free, n + 1)
                    sp.dma_start(xs[:, :], kit.tokc[rows_T, 0:D]).then_inc(in_loaded, 16)
                    sp.dma_start(zo[:, 0, :], kit.zvo[rows_T, 0:D]).then_inc(in_loaded, 16)
                    sp.dma_start(zo[:, 1, :], kit.zvo[rows_T, 2 * D:3 * D]).then_inc(in_loaded, 16)
                sp.wait_ge(h_free[j], m + 1)
                sp.dma_start(h[j][:, :], src[:, bass.ds(t, 1), :].rearrange("p a d -> p (a d)")).then_inc(h_loaded[j], 16)

            tiles_of(sp, load)

        @block.gpsimd
        def _(pool):
            G = nc.gpsimd
            for j in range(2):
                pool.sem_inc(h_free[j], 1)
            if even:
                pool.wait_ge(skip_loaded, 16)

            def prepare(T, n):
                yrow = src_y[:, bass.ds(T, 1), :].rearrange("p a x -> p (a x)")
                pool.wait_ge(in_loaded, n * 48 + 48)
                G.tensor_tensor(xs[:, :].rearrange("p (h x) -> p h x", x=SSD_P), xs[:, :].rearrange("p (h x) -> p h x", x=SSD_P),
                                dsk[:, :].unsqueeze(2).to_broadcast([P, SSD_HEADS, SSD_P]), ALU.mult).then_inc(skip_ready, 1)
                pool.wait_ge(skip_ready, n * 2 + 1)
                G.tensor_tensor(yrow, yrow, xs[:, :], ALU.add).then_inc(skip_ready, 1)

            def step(T, n, m, j, src, t, s, more):
                yrow = src_y[:, bass.ds(T, 1), :].rearrange("p a x -> p (a x)")
                if even and more:
                    prepare(T + 1, n + 1)
                pool.wait_ge(h_loaded[j], m * 16 + 16)
                pool.wait_ge(gated, n + 1)
                G.tensor_tensor(h[j][:, :], h[j][:, :], n1[:, :], ALU.add).then_inc(h_ready, 1)
                pool.wait_ge(h_ready, n + 1)
                pool.dma_start(h_out[bass.ds(T * P, P), :], h[j][:, :]).then_inc(h_stored[j], 16)
                pool.wait_ge(n_ready, n + 1)
                pool.wait_ge(s2_ready, len(groups))
                G.tensor_tensor(n1[:, :], n1[:, :], sc2[s][:, :], ALU.mult).then_inc(tm_ready, 1)
                wait_alone(pool, t_ready, n + 1, passed)
                pool.dma_start(kit.t[bass.ds(T * P, P), :], yrow).then_inc(t_stored, 16)
                pool.wait_ge(h_stored[j], m * 16 + 16)
                pool.sem_inc(h_free[j], 1)

            if even:
                prepare(first, 0)
            tiles_of(pool, step)
            pool.wait_ge(t_stored, 16 * count)

        @block.scalar
        def _(act):
            ACTV = nc.scalar.activation
            if even:
                act.sem_inc(in_free, 1)
                act.wait_ge(in_loaded, 48)
            for c in range(2):
                hk = K // 2
                act.dma_start(w[:, c * hk:(c + 1) * hk, :], w_out.rearrange("(k p) n -> p k n", p=P)[:, c * hk:(c + 1) * hk, :]).then_inc(w_loaded[c], 16)
            rows = [(w2[:, :], A["norm2_w"][layer].partition_broadcast(P))]
            for src, tile0, pairs, cond, s, base in groups:
                for dst, c in ((gate[s], 2), (sh2[s], 3), (sc2[s], 4)):
                    rows.append((dst[:, :], kit.mod[cond, base_mod + c * D:base_mod + (c + 1) * D].partition_broadcast(P)))
            for dst, src in rows:
                act.dma_start(dst, src).then_inc(rows_loaded, 16)
            act.dma_start(wr[:, :, 0:4], A["moe_w_group"][layer].rearrange("(k p) n -> p k n", p=P)).then_inc(rows_loaded, 16)
            act.dma_start(wr[:, :, 4:20], A["moe_w_expert"][layer].rearrange("(k p) n -> p k n", p=P)).then_inc(rows_loaded, 16)

            def prepare(T, n):
                yrow = src_y[:, bass.ds(T, 1), :].rearrange("p a x -> p (a x)")
                hrow = kit.hacc[:, bass.ds(T, 1), :].rearrange("p a x -> p (a x)")
                act.wait_ge(in_loaded, n * 48 + 48)
                for g in range(NG_M):
                    ACTV(junk[:, 0:W_M], hrow[:, g * W_M:(g + 1) * W_M], ACT.Square, accum_out=ss[:, 2 + g:3 + g]).then_inc(junked, 1)
                    act.wait_ge(junked, n * JUNKS + g + 1)
                ACTV(zo[:, 1, :], zo[:, 1, :], ACT.Sigmoid)
                ACTV(zo[:, 0, :], zo[:, 0, :], ACT.Silu).then_inc(gates_ready, 1)
                act.wait_ge(yg_ready, n + 1)
                for g in range(NG_S):
                    ACTV(junk[:, 0:W_S], yrow[:, g * W_S:(g + 1) * W_S], ACT.Square, accum_out=ss[:, g:g + 1]).then_inc(junked, 1)
                    act.wait_ge(junked, n * JUNKS + NG_M + g + 1)
                act.sem_inc(ss_ready, 1)
                act.wait_ge(rs_half, n + 1)
                nc.scalar.sqrt(rs[:, 0:6], ss[:, 0:6]).then_inc(rs_ready, 1)

            def take_turned(n):
                act.wait_ge(turned, n + 1)
                nc.scalar.copy(yT[:, 0:K // 2, :], ps_t[:, 0:K // 2, :]).then_inc(yT_act, 1)

            def step(T, n, m, j, src, t, s, more):
                if even and more:
                    prepare(T + 1, n + 1)
                if more:
                    take_turned(n + 1)
                act.wait_ge(h_ready, n + 1)
                ACTV(junk[:, :], h[j][:, :], ACT.Square, accum_out=s2[:, 0:1]).then_inc(h_junked, 1)
                act.wait_ge(h_junked, n + 1)
                act.sem_inc(sq_ready, 1)
                act.wait_ge(r2_half, n + 1)
                nc.scalar.sqrt(r2[:, 0:1], s2[:, 1:2]).then_inc(r2_ready, 1)
                act.wait_ge(r2_ready, n + 1)
                ACTV(n1[:, :], h[j][:, :], ACT.Copy, scale=r2[:, 0:1]).then_inc(n_ready, 1)

            if even:
                prepare(first, 0)
            take_turned(0)
            if even:
                act.wait_ge(w_loaded[0], 16)
                for k in range(K // 2):
                    last = ACTV(w[:, k, :], w[:, k, :], ACT.Copy, scale=kit.pcol[:, COL_SSD + k:COL_SSD + k + 1])
                last.then_inc(w_ready, 1)
            tiles_of(act, step)
            for n in range(count):
                half = slice(n % 2 * KD, n % 2 * KD + KD)
                act.wait_ge(t_turned, n + 1)
                if n >= 2:
                    act.wait_ge(logits_done, n - 1)
                nc.scalar.copy(tT[:, half, :], ps_t[:, half, :]).then_inc(tT_ready, 1)

        @block.vector
        def _(dve):
            V = nc.vector
            TT, TS, STT = V.tensor_tensor, V.tensor_scalar, V.scalar_tensor_tensor
            ch = Chain(dve, chain_v)
            LINKS = (3 if even else 0) + 1

            def prepare(T, n):
                yrow = src_y[:, bass.ds(T, 1), :].rearrange("p a x -> p (a x)")
                if even:
                    hrow = kit.hacc[:, bass.ds(T, 1), :].rearrange("p a x -> p (a x)")
                    dve.wait_ge(gates_ready, n + 1)
                    dve.wait_ge(skip_ready, n * 2 + 2)
                    TT(yrow, yrow, zo[:, 0, :], ALU.mult).then_inc(yg_ready, 1)
                    dve.wait_ge(ss_ready, n + 1)
                    ch(TS(ss[:, 0:2], ss[:, 0:2], 1.0 / W_S, EPS, ALU.mult, ALU.add))
                    ch(TS(ss[:, 2:6], ss[:, 2:6], 1.0 / W_M, EPS, ALU.mult, ALU.add))
                    V.reciprocal(ss[:, 0:6], ss[:, 0:6]).then_inc(rs_half, 1)
                    dve.wait_ge(rs_ready, n + 1)
                    for g in range(NG_S):
                        TS(yrow[:, g * W_S:(g + 1) * W_S], yrow[:, g * W_S:(g + 1) * W_S], rs[:, g:g + 1], None, ALU.mult)
                    for g in range(NG_M):
                        cols = slice(g * W_M, (g + 1) * W_M)
                        last = STT(hrow[:, cols], hrow[:, cols], rs[:, 2 + g:3 + g], zo[:, 1, cols], ALU.mult, ALU.mult)
                    ch(last)
                    dve.sem_inc(in_free, 1)
                    wait_alone(dve, mix_free, n + 1, passed)
                    V.tensor_copy(mix[:, 0:D], yrow)
                    V.tensor_copy(mix[:, D:2 * D], hrow).then_inc(mix_ready, 1)
                else:
                    wait_alone(dve, mix_free, n + 1, passed)
                    V.tensor_copy(mix[:, 0:D], yrow).then_inc(mix_ready, 1)

            def take_turned(n):
                dve.wait_ge(turned, n + 1)
                V.tensor_copy(yT[:, K // 2:K, :], ps_t[:, K // 2:K, :]).then_inc(yT_dve, 1)

            def step(T, n, m, j, src, t, s, more):
                yrow = src_y[:, bass.ds(T, 1), :].rearrange("p a x -> p (a x)")
                if more:
                    prepare(T + 1, n + 1)
                dve.wait_ge(y_ready, n + 1)
                TT(n1[:, :], ps_y[:, :], gate[s][:, :], ALU.mult).then_inc(gated, 1)
                dve.wait_ge(gated, n + 1)
                dve.sem_inc(y_taken, 1)
                if more:
                    take_turned(n + 1)
                dve.wait_ge(sq_ready, n + 1)
                ch(TS(s2[:, 0:1], s2[:, 0:1], 1.0 / D, EPS, ALU.mult, ALU.add))
                V.reciprocal(s2[:, 1:2], s2[:, 0:1]).then_inc(r2_half, 1)
                dve.wait_ge(tm_ready, n + 1)
                TT(yrow, n1[:, :], sh2[s][:, :], ALU.add).then_inc(t_ready, 1)
                dve.wait_ge(t_ready, n + 1)

            prepare(first, 0)
            take_turned(0)
            if even:
                dve.wait_ge(w_loaded[1], 16)
                for k in range(K // 2, K):
                    last = TS(w[:, k, :], w[:, k, :], kit.pcol[:, COL_SSD + k:COL_SSD + k + 1], None, ALU.mult)
                last.then_inc(w_ready, 1)
            dve.wait_ge(rows_loaded, ROWS)
            for s in range(len(groups)):
                STT(sc2[s][:, :], sc2[s][:, :], 1.0, w2[:, :], ALU.add, ALU.mult).then_inc(s2_ready, 1)
            tiles_of(dve, step, ch, LINKS)
            for n in range(count):
                dve.wait_ge(logits_done, n + 1)
                V.tensor_copy(kit.logits[:, n, :], ps_r[:, 0:20]).then_inc(logits_out, 1)

        @block.tensor
        def _(pe):
            pe.sem_inc(mix_free, 1)
            pe.sem_inc(y_taken, 1)

            def turn(n):
                pe.wait_ge(mix_ready, n + 1)
                for k in range(K):
                    last = nc.tensor.transpose(ps_t[:, k, :], mix[:, k * P:(k + 1) * P], consts[:, 0:P])
                last.then_inc(turned, 1)
                pe.wait_ge(turned, n + 1)
                pe.sem_inc(mix_free, 1)

            def step(T, n, m, j, src, t, s, more):
                pe.wait_ge(yT_act, n + 1)
                pe.wait_ge(yT_dve, n + 1)
                pe.wait_ge(y_taken, n + 1)
                for c in range(2):
                    for k in range(K):
                        last = nc.tensor.matmul(ps_y[:, c * BANK:(c + 1) * BANK], yT[:, k, :], w[:, k, c * BANK:(c + 1) * BANK],
                                                start=(k == 0), stop=(k == K - 1))
                last.then_inc(y_ready, 1)
                if more:
                    turn(n + 1)

            turn(0)
            if even:
                pe.wait_ge(w_ready, 2)
            else:
                for c in range(2):
                    pe.wait_ge(w_loaded[c], 16)
            tiles_of(pe, step)
            pe.wait_ge(rows_loaded, ROWS)
            def turn_t(n):
                pe.wait_ge(t_ready, n + 1)
                if n >= 2:
                    pe.wait_ge(tT_ready, n - 1)
                for k in range(KD):
                    last = nc.tensor.transpose(ps_t[:, n % 2 * KD + k, :], src_y[:, first + n, k * P:(k + 1) * P], consts[:, 0:P])
                last.then_inc(t_turned, 1)

            turn_t(0)
            for n in range(count):
                if n + 1 < count:
                    turn_t(n + 1)
                pe.wait_ge(tT_ready, n + 1)
                if n:
                    pe.wait_ge(logits_out, n)
                for k in range(KD):
                    last = nc.tensor.matmul(ps_r[:, 0:20], tT[:, n % 2 * KD + k, :], wr[:, k, :], start=(k == 0), stop=(k == KD - 1))
                last.then_inc(logits_done, 1)


NGRP, EPG, FF = 4, 4, 256
NEXP = NGRP * EPG
MAXCH = 28
NCK = MAXCH + 2
R_TIE, R_TOK, R_CHUNK, R_THR, R_PAIR, NROUTE = 0, 4, 10, 10 + NCK, 16 + NCK, 30 + NCK


def host_route():
    r = np.zeros((P, NROUTE), np.float32)
    r[:, R_TIE:R_TIE + 4] = [4, 3, 2, 1]
    r[:, R_TOK:R_TOK + NT] = np.arange(P)[:, None] + P * np.arange(NT)[None, :]
    r[:, R_CHUNK:R_CHUNK + NCK] = np.arange(NCK)
    r[:, R_THR:R_THR + NT] = P * np.arange(NT)
    r[:, R_PAIR:R_PAIR + MAXCH // 2] = 2 * np.arange(MAXCH // 2)
    return r


def phase_route(kit, layer, tile0, N):
    nc, consts = kit.nc, kit.consts
    with ExitStack() as st:
        sb = lambda n, s, d=F32: st.enter_context(nc.sbuf_tensor(f"rt{layer}_{n}", s, d))
        tab, zero = sb("tab", [P, NROUTE]), sb("zero", [P, NCK], I32)
        top, tot, pg, m1, m2, e2 = (sb(n, [P, N, 1]) for n in ("top", "tot", "pg", "m1", "m2", "e2"))
        tie, ohg, ex, sel, oh1, oh2, rest = (sb(n, [P, N, 4]) for n in ("tie", "ohg", "ex", "sel", "oh1", "oh2", "rest"))
        prod = sb("prod", [P, N, 4, 4])
        full = [sb(f"full{a}", [P, N, NEXP]) for a in range(2)]
        slots = sb("slots", [P, N, NEXP])
        both, strict_b, ones_b = sb("both", [P, N, NEXP], BF16), sb("strict_b", [P, P], BF16), sb("ones_b", [P, P], BF16)
        cnt, nch, end, base, ones16 = (sb(n, [P, NEXP]) for n in ("cnt", "nch", "end", "base", "ones16"))
        over = sb("over", [P, NEXP, NT])
        cmp, cexp = sb("cmp", [P, NCK, NEXP]), sb("cexp", [P, NCK])
        posf = sb("posf", [P, N, 2])
        pair, npair = sb("pair", [P, MAXCH // 2]), sb("npair", [P, 1])
        tok_i = sb("tok_i", [P, NT], I32)
        list_i, list_f = sb("list_i", [NCK, P], I32), sb("list_f", [NCK, P])
        ps_list = st.enter_context(nc.psum_tensor(f"rt{layer}_ps_list", [P, BANK], F32))
        ps_rank = st.enter_context(nc.psum_tensor(f"rt{layer}_ps_rank", [P, BANK], F32))
        ps_tot = st.enter_context(nc.psum_tensor(f"rt{layer}_ps_tot", [P, BANK], F32))
        S = lambda n: kit.sem(f"rt{layer}_" + n)
        tab_loaded, cleared, zeroed, exp_asked, exp_given, chosen, counted, placed, scattered, listed = (
            S(n) for n in ("tab_loaded", "cleared", "zeroed", "exp_asked", "exp_given", "chosen", "counted", "placed", "scattered", "listed"))
        list_ready, list_turned, chain_v = S("list_ready"), S("list_turned"), S("chain_v")
        block = st.enter_context(nc.Block())

        @block.sync
        def _(sp):
            sp.dma_start(tab[:, :], kit.A["route"]).then_inc(tab_loaded, 16)
            sp.wait_ge(cleared, 1)
            sp.dma_start(kit.slot_tok.rearrange("(p c) o -> p (c o)", p=P), zero[:, :]).then_inc(zeroed, 16)
            sp.wait_ge(scattered, 16 * 2 * N)
            sp.dma_start(list_i[:, :], kit.slot_tok.rearrange("(c p) o -> c (p o)", p=P)).then_inc(listed, 16)

        @block.gpsimd
        def _(pool):
            nc.gpsimd.memset(zero[:, :], 0).then_inc(cleared, 1)
            pool.wait_ge(placed, 1)
            pool.wait_ge(zeroed, 16)
            for n in range(N):
                for a in range(2):
                    pool.indirect_dma_start(out=kit.slot_tok, out_offset=bass.IndirectOffsetOnAxis(ap=kit.pos[:, n, a:a + 1], axis=0),
                                            in_=tok_i[:, tile0 + n:tile0 + n + 1], in_offset=None).then_inc(scattered, 16)
            pool.wait_ge(scattered, 16 * 2 * N)

        @block.scalar
        def _(act):
            act.wait_ge(exp_asked, 1)
            nc.scalar.activation(ex[:, :, :], ex[:, :, :], ACT.Exp).then_inc(exp_given, 1)
            act.wait_ge(exp_asked, 2)
            nc.scalar.activation(e2[:, :, :], e2[:, :, :], ACT.Exp).then_inc(exp_given, 1)

        @block.tensor
        def _(pe):
            pe.wait_ge(chosen, 1)
            for n in range(N):
                for q in range(n):
                    nc.tensor.matmul(ps_rank[:, n * NEXP:(n + 1) * NEXP], ones_b[:, :], both[:, q, :], start=(q == 0), stop=False)
                nc.tensor.matmul(ps_rank[:, n * NEXP:(n + 1) * NEXP], strict_b[:, :], both[:, n, :], start=(n == 0), stop=True)
            for n in range(N):
                last = nc.tensor.matmul(ps_tot[:, 0:NEXP], ones_b[:, :], both[:, n, :], start=(n == 0), stop=(n == N - 1))
            last.then_inc(counted, 1)
            pe.wait_ge(list_ready, 1)
            nc.tensor.transpose(ps_list[:, 0:NCK], list_f[:, :], consts[0:NCK, 0:NCK]).then_inc(list_turned, 1)

        @block.vector
        def _(dve):
            V = nc.vector
            TT, TS, STT, RED = V.tensor_tensor, V.tensor_scalar, V.scalar_tensor_tensor, V.tensor_reduce
            ch = Chain(dve, chain_v)
            gl, el = kit.logits[:, 0:N, 0:4], kit.logits[:, 0:N, 4:20]
            ch(V.tensor_copy(strict_b[:, :], consts[:, C_STRICT:C_STRICT + P]))
            ch(V.tensor_copy(ones_b[:, :], consts[:, C_ONE:C_ONE + P]))
            ch(V.memset(ones16[:, :], 1.0))
            dve.wait_ge(tab_loaded, 16)

            def first_of(oh, x, m):
                ch(TT(tie[:, :, :], x, m[:, :, :].to_broadcast([P, N, 4]), ALU.is_equal))
                ch(TT(tie[:, :, :], tie[:, :, :], tab[:, R_TIE:R_TIE + 4].unsqueeze(1).to_broadcast([P, N, 4]), ALU.mult))
                ch(RED(tot[:, :, 0], tie[:, :, :], AX.X, ALU.max))
                ch(TT(oh[:, :, :], tie[:, :, :], tot[:, :, :].to_broadcast([P, N, 4]), ALU.is_equal))

            ch(RED(top[:, :, 0], gl, AX.X, ALU.max))
            first_of(ohg, gl, top)
            ch(TT(ex[:, :, :], gl, top[:, :, :].to_broadcast([P, N, 4]), ALU.subtract))
            dve.sem_inc(exp_asked, 1)
            ch(TT(prod[:, :, :, :], el.rearrange("p n (g j) -> p n g j", j=4), ohg[:, :, :].unsqueeze(3).to_broadcast([P, N, 4, 4]), ALU.mult))
            ch(RED(sel[:, :, :], prod[:, :, :, :].rearrange("p n g j -> p n j g"), AX.X, ALU.add))
            ch(RED(m1[:, :, 0], sel[:, :, :], AX.X, ALU.max))
            first_of(oh1, sel[:, :, :], m1)
            ch(STT(rest[:, :, :], oh1[:, :, :], NEG, sel[:, :, :], ALU.mult, ALU.add))
            ch(RED(m2[:, :, 0], rest[:, :, :], AX.X, ALU.max))
            first_of(oh2, rest[:, :, :], m2)
            ch(TT(e2[:, :, :], m2[:, :, :], m1[:, :, :], ALU.subtract))
            dve.sem_inc(exp_asked, 1)
            for a, oh in enumerate((oh1, oh2)):
                ch(TT(full[a][:, :, :].rearrange("p n (g j) -> p n g j", j=4), ohg[:, :, :].unsqueeze(3).to_broadcast([P, N, 4, 4]),
                      oh[:, :, :].unsqueeze(2).to_broadcast([P, N, 4, 4]), ALU.mult))
            TT(both[:, :, :], full[0][:, :, :], full[1][:, :, :], ALU.add).then_inc(chosen, 1)
            dve.wait_ge(exp_given, 2)
            ch(RED(pg[:, :, 0], ex[:, :, :], AX.X, ALU.add))
            ch(TS(m1[:, :, :], e2[:, :, :], 1.0, None, ALU.add))
            ch(TT(pg[:, :, :], pg[:, :, :], m1[:, :, :], ALU.mult))
            ch(V.reciprocal(kit.wts[:, 0:N, 0:1], pg[:, :, :]))
            ch(TT(kit.wts[:, 0:N, 1:2], kit.wts[:, 0:N, 0:1], e2[:, :, :], ALU.mult))
            dve.wait_ge(counted, 1)
            ch(V.tensor_copy(cnt[:, :], ps_tot[:, 0:NEXP]))
            ch(TT(over[:, :, :], cnt[:, :].unsqueeze(2).to_broadcast([P, NEXP, NT]), tab[:, R_THR:R_THR + NT].unsqueeze(1).to_broadcast([P, NEXP, NT]), ALU.is_gt))
            ch(RED(nch[:, :], over[:, :, :], AX.X, ALU.add))
            ch(V.tensor_tensor_scan(end[:, :], ones16[:, :], nch[:, :], 0.0, ALU.mult, ALU.add))
            ch(TT(base[:, :], end[:, :], nch[:, :], ALU.subtract))
            ch(TS(base[:, :], base[:, :], float(P), None, ALU.mult))
            ch(TT(slots[:, :, :], ps_rank[:, 0:N * NEXP].rearrange("p (n e) -> p n e", e=NEXP), base[:, :].unsqueeze(1).to_broadcast([P, N, NEXP]), ALU.add))
            for a in range(2):
                ch(TT(full[a][:, :, :], full[a][:, :, :], slots[:, :, :], ALU.mult))
                ch(RED(posf[:, :, a], full[a][:, :, :], AX.X, ALU.add))
            ch(V.tensor_copy(kit.pos[:, 0:N, :], posf[:, :, :]))
            V.tensor_copy(tok_i[:, :], tab[:, R_TOK:R_TOK + NT]).then_inc(placed, 1)
            ch(TT(cmp[:, :, :], tab[:, R_CHUNK:R_CHUNK + NCK].unsqueeze(2).to_broadcast([P, NCK, NEXP]), end[:, :].unsqueeze(1).to_broadcast([P, NCK, NEXP]), ALU.is_ge))
            ch(RED(cexp[:, :], cmp[:, :, :], AX.X, ALU.add))
            ch(TS(cexp[:, :], cexp[:, :], float(NEXP - 1), None, ALU.min))
            ch(V.tensor_copy(kit.plan[:, 0:NCK], cexp[:, :]))
            ch(TT(pair[:, :], end[:, NEXP - 1:NEXP].to_broadcast([P, MAXCH // 2]), tab[:, R_PAIR:R_PAIR + MAXCH // 2], ALU.is_gt))
            ch(RED(npair[:, :], pair[:, :], AX.X, ALU.add))
            ch(V.tensor_copy(kit.plan[:, NCK:NCK + 1], npair[:, :]))
            dve.wait_ge(listed, 16)
            V.tensor_copy(list_f[:, :], list_i[:, :]).then_inc(list_ready, 1)
            dve.wait_ge(list_turned, 1)
            V.tensor_copy(kit.slots_in[:, :], ps_list[:, 0:NCK])


def phase_experts(kit, layer, N):
    nc, A, consts = kit.nc, kit.A, kit.consts
    pairs_max = (N * P * 2 + NEXP * (P - 1)) // P // 2 + 1
    with ExitStack() as st:
        sb = lambda n, s, d=F32: st.enter_context(nc.sbuf_tensor(f"ex{layer}_{n}", s, d))
        ps = lambda n, s: st.enter_context(nc.psum_tensor(f"ex{layer}_{n}", s, F32))
        two = lambda n, s, d=F32: [sb(f"{n}{j}", s, d) for j in range(2)]
        wgu, wd = two("wgu", [P, KD, 2 * FF]), two("wd", [P, FF // P, D])
        xg, xT, hid, hT, y = two("xg", [P, D]), two("xT", [P, KD, P]), two("hid", [P, FF]), two("hT", [P, FF // P, P]), two("y", [P, D])
        idx = two("idx", [P, 1], I32)
        ps_gu = [ps(f"ps_gu{j}", [P, BANK]) for j in range(2)]
        ps_x, ps_h, ps_d = ps("ps_x", [P, KD, P]), ps("ps_h", [P, BANK]), ps("ps_d", [P, D])
        S = lambda n: kit.sem(f"ex{layer}_" + n)
        passed = S("passed")
        wgu_loaded, wd_loaded, x_loaded, y_stored = ([S(f"{n}{j}") for j in range(2)] for n in ("wgu_loaded", "wd_loaded", "x_loaded", "y_stored"))
        wgu_free, wd_free, x_free, y_free = ([S(f"{n}{j}") for j in range(2)] for n in ("wgu_free", "wd_free", "x_free", "y_free"))
        idx_ready, gu_ready, silu_ready, hid_ready, x_turned, xT_act, xT_dve, h_turned, hT_ready, d_ready, y_act, y_dve = (
            S(n) for n in ("idx_ready", "gu_ready", "silu_ready", "hid_ready", "x_turned", "xT_act", "xT_dve", "h_turned", "hT_ready", "d_ready", "y_act", "y_dve"))
        w_views = [A[n][layer].rearrange("g e (k p) f -> (g e) p k f", p=P) for n in ("moe_w_gate", "moe_w_up", "moe_w_down")]
        block = st.enter_context(nc.Block())

        def pairs(eng):
            return eng.value_load(kit.plan[0:1, NCK:NCK + 1], min_val=1, max_val=pairs_max)

        @block.sync
        def _(sp):
            with sp.Fori(0, pairs(sp)) as i:
                for s in range(2):
                    e = sp.value_load(kit.plan[0:1, bass.ds(i * 2 + s, 1)], min_val=0, max_val=NEXP - 1)
                    sp.wait_ge(wgu_free[s], i + 1)
                    for c in range(2):
                        sp.dma_start(wgu[s][:, :, c * FF:(c + 1) * FF], w_views[c][bass.ds(e, 1)].rearrange("a p k f -> p (a k) f")).then_inc(wgu_loaded[s], 16)
                    sp.wait_ge(wd_free[s], i + 1)
                    sp.dma_start(wd[s][:, :, :], w_views[2][bass.ds(e, 1)].rearrange("a p k f -> p (a k) f")).then_inc(wd_loaded[s], 16)

        @block.gpsimd
        def _(pool):
            def gather(c, s, m):
                pool.wait_ge(x_free[s], m)
                nc.gpsimd.tensor_copy(idx[s][:, :], kit.slots_in[:, bass.ds(c, 1)]).then_inc(idx_ready, 1)
                wait_alone(pool, idx_ready, c + 1, passed)
                pool.indirect_dma_start(out=xg[s][:, :], out_offset=None, in_=kit.t,
                                        in_offset=bass.IndirectOffsetOnAxis(ap=idx[s][:, 0:1], axis=0)).then_inc(x_loaded[s], 16)

            gather(0, 0, 1)
            with pool.Fori(0, pairs(pool)) as i:
                gather(i * 2 + 1, 1, i + 1)
                gather(i * 2 + 2, 0, i + 2)
            n = pairs(pool)
            pool.wait_ge(x_loaded[0], n * 16 + 16)

        @block.tensor
        def _(pe):
            for s in range(2):
                for f in (wgu_free, wd_free, x_free):
                    pe.sem_inc(f[s], 1)

            def turn_x(c, s, m):
                pe.wait_ge(x_loaded[s], m * 16)
                pe.wait_ge(xT_act, c + 1)
                pe.wait_ge(xT_dve, c + 1)
                for k in range(KD):
                    last = nc.tensor.transpose(ps_x[:, k, :], xg[s][:, k * P:(k + 1) * P], consts[:, 0:P])
                last.then_inc(x_turned, 1)

            turn_x(0, 0, 1)
            pe.wait_ge(x_turned, 1)
            pe.sem_inc(x_free[0], 1)
            with pe.Fori(0, pairs(pe)) as i:
                for s in range(2):
                    c = i * 2 + s
                    pe.wait_ge(wgu_loaded[s], i * 32 + 32)
                    pe.wait_ge(xT_act, c + 2)
                    pe.wait_ge(xT_dve, c + 2)
                    for k in range(KD):
                        last = nc.tensor.matmul(ps_gu[s][:, :], xT[s][:, k, :], wgu[s][:, k, :], start=(k == 0), stop=(k == KD - 1))
                    last.then_inc(gu_ready, 1)
                    turn_x(c + 1, 1 - s, i + 1 + s)
                    pe.wait_ge(x_turned, c + 2)
                    pe.sem_inc(wgu_free[s], 1)
                    pe.sem_inc(x_free[1 - s], 1)
                    pe.wait_ge(hid_ready, c + 1)
                    for k in range(FF // P):
                        last = nc.tensor.transpose(ps_h[:, k * P:(k + 1) * P], hid[s][:, k * P:(k + 1) * P], consts[:, 0:P])
                    last.then_inc(h_turned, 1)
                    pe.wait_ge(wd_loaded[s], i * 16 + 16)
                    pe.wait_ge(hT_ready, c + 1)
                    pe.wait_ge(y_act, c + 1)
                    pe.wait_ge(y_dve, c + 1)
                    for h in range(2):
                        for k in range(FF // P):
                            last = nc.tensor.matmul(ps_d[:, h * BANK:(h + 1) * BANK], hT[s][:, k, :], wd[s][:, k, h * BANK:(h + 1) * BANK],
                                                    start=(k == 0), stop=(k == FF // P - 1))
                    last.then_inc(d_ready, 1)
                    pe.wait_ge(d_ready, c + 1)
                    pe.sem_inc(wd_free[s], 1)

        @block.scalar
        def _(act):
            act.sem_inc(xT_act, 1)
            act.sem_inc(y_act, 1)
            for s in range(2):
                act.sem_inc(y_free[s], 1)

            def take_x(c, s):
                act.wait_ge(x_turned, c + 1)
                nc.scalar.copy(xT[s][:, 0:KD // 2, :], ps_x[:, 0:KD // 2, :]).then_inc(xT_act, 1)

            take_x(0, 0)
            with act.Fori(0, pairs(act)) as i:
                for s in range(2):
                    c = i * 2 + s
                    act.wait_ge(gu_ready, c + 1)
                    nc.scalar.activation(hid[s][:, :], ps_gu[s][:, 0:FF], ACT.Silu).then_inc(silu_ready, 1)
                    take_x(c + 1, 1 - s)
                    act.wait_ge(d_ready, c + 1)
                    act.wait_ge(y_free[s], i + 1)
                    nc.scalar.copy(y[s][:, 0:BANK], ps_d[:, 0:BANK]).then_inc(y_act, 1)
                    act.wait_ge(y_act, c + 2)
                    act.wait_ge(y_dve, c + 2)
                    act.dma_start(kit.y[bass.ds(c * P, P), :], y[s][:, :]).then_inc(y_stored[s], 16)
                    if s == 1:
                        for r in range(2):
                            act.wait_ge(y_stored[r], i * 16 + 16)
                            act.sem_inc(y_free[r], 1)

        @block.vector
        def _(dve):
            V = nc.vector
            dve.sem_inc(xT_dve, 1)
            dve.sem_inc(y_dve, 1)

            def take_x(c, s):
                dve.wait_ge(x_turned, c + 1)
                V.tensor_copy(xT[s][:, KD // 2:KD, :], ps_x[:, KD // 2:KD, :]).then_inc(xT_dve, 1)

            take_x(0, 0)
            with dve.Fori(0, pairs(dve)) as i:
                for s in range(2):
                    c = i * 2 + s
                    dve.wait_ge(silu_ready, c + 1)
                    V.tensor_tensor(hid[s][:, :], hid[s][:, :], ps_gu[s][:, FF:2 * FF], ALU.mult).then_inc(hid_ready, 1)
                    take_x(c + 1, 1 - s)
                    dve.wait_ge(h_turned, c + 1)
                    V.tensor_copy(hT[s][:, :, :], ps_h[:, 0:FF].rearrange("p (k q) -> p k q", q=P)).then_inc(hT_ready, 1)
                    dve.wait_ge(d_ready, c + 1)
                    dve.wait_ge(y_free[s], i + 1)
                    V.tensor_copy(y[s][:, BANK:D], ps_d[:, BANK:D]).then_inc(y_dve, 1)


def phase_combine(kit, layer, h_in, h_out, sources, final):
    nc, A, consts = kit.nc, kit.A, kit.consts
    with ExitStack() as st:
        sb = lambda n, s, d=F32: st.enter_context(nc.sbuf_tensor(f"cb{layer}_{n}", s, d))
        two = lambda n, s, d=F32: [sb(f"{n}{j}", s, d) for j in range(2)]
        x, ya, yb, xn = two("x", [P, D]), two("ya", [P, D]), two("yb", [P, D]), two("xn", [P, D])
        idx = two("idx", [P, 2], I32)
        ss, rs = sb("ss", [P, 2, 2]), sb("rs", [P, 2])
        junk = sb("junk", [P, D])
        gate = [sb(f"gate{s}", [P, D]) for s in range(len(sources))]
        fw = sb("fw", [P, D]) if final else None
        ps = [st.enter_context(nc.psum_tensor(f"cb{layer}_ps{j}", [P, KD, P], F32)) for j in range(2)]
        S = lambda n: kit.sem(f"cb{layer}_" + n)
        passed = S("passed")
        rows_loaded, x_loaded, y_loaded, h_stored, o_stored = S("rows_loaded"), *([S(f"{n}{j}") for j in range(2)] for n in ("x_loaded", "y_loaded", "h_stored", "o_stored"))
        x_free, idx_ready, h_ready, sq_ready, r_half, rs_ready, xn_ready, turned, act_out, dve_out, read = (
            S(n) for n in ("x_free", "idx_ready", "h_ready", "sq_ready", "r_half", "rs_ready", "xn_ready", "turned", "act_out", "dve_out", "read"))
        chain_v = S("chain_v")
        groups, before = [], 0
        for s, (tile0, tiles, cond) in enumerate(sources):
            groups.append((tile0, tiles // 2, cond, s, before))
            before += tiles
        count = before
        first = sources[0][0]
        gate_at = layer * 6 * D + 5 * D
        block = st.enter_context(nc.Block())

        def tiles_of(eng, body, ch=None, links=0):
            for tile0, pairs, cond, s, base in groups:
                with eng.Fori(0, pairs) as i:
                    if ch:
                        ch.enter(i, 2 * links)
                    for j in range(2):
                        body(i * 2 + (tile0 + j), i * 2 + (base + j), i + base // 2, j, cond, s)
                    if ch:
                        ch.leave(pairs)

        @block.sync
        def _(sp):
            for tile0, pairs, cond, s, base in groups:
                sp.dma_start(gate[s][:, :], kit.mod[cond, gate_at:gate_at + D].partition_broadcast(P)).then_inc(rows_loaded, 16)
            if final:
                sp.dma_start(fw[:, :], A["final_norm_w"].partition_broadcast(P)).then_inc(rows_loaded, 16)

            def load(T, n, m, j, cond, s):
                sp.wait_ge(x_free, n + 1)
                sp.dma_start(x[j][:, :], h_in[bass.ds(T * P, P), :]).then_inc(x_loaded[j], 16)

            tiles_of(sp, load)

        @block.gpsimd
        def _(pool):
            pool.sem_inc(x_free, 1)
            pool.sem_inc(x_free, 1)
            out_rows = kit.out[0] if final else h_out

            def step(T, n, m, j, cond, s):
                pool.wait_ge(x_free, n + 1)
                nc.gpsimd.tensor_copy(idx[j][:, :], kit.pos[:, bass.ds(n, 1), :].rearrange("p a b -> p (a b)")).then_inc(idx_ready, 1)
                wait_alone(pool, idx_ready, n + 1, passed)
                for a, dst in enumerate((ya, yb)):
                    pool.indirect_dma_start(out=dst[j][:, :], out_offset=None, in_=kit.y,
                                            in_offset=bass.IndirectOffsetOnAxis(ap=idx[j][:, a:a + 1], axis=0)).then_inc(y_loaded[j], 16)

            def finish(T, n, m, j, cond, s):
                if final:
                    pool.wait_ge(xn_ready, n + 1)
                    pool.dma_start(out_rows[bass.ds((T - first) * P, P), :], xn[j][:, :]).then_inc(o_stored[j], 16)
                    pool.wait_ge(o_stored[j], m * 16 + 16)
                else:
                    pool.wait_ge(h_ready, n + 1)
                    pool.dma_start(out_rows[bass.ds(T * P, P), :], x[j][:, :]).then_inc(h_stored[j], 16)
                    pool.wait_ge(h_stored[j], m * 16 + 16)
                    pool.wait_ge(xn_ready, n + 1)
                pool.sem_inc(x_free, 1)

            for tile0, pairs, cond, s, base in groups:
                with pool.Fori(0, pairs) as i:
                    for f in (step, finish):
                        for j in range(2):
                            f(i * 2 + (tile0 + j), i * 2 + (base + j), i + base // 2, j, cond, s)

        @block.scalar
        def _(act):
            ACTV = nc.scalar.activation

            def step(T, n, m, j, cond, s):
                act.wait_ge(h_ready, n + 1)
                ACTV(junk[:, :], x[j][:, :], ACT.Square, accum_out=ss[:, j, 0:1]).then_inc(sq_ready, 1)
                act.wait_ge(r_half, n + 1)
                nc.scalar.sqrt(rs[:, j:j + 1], ss[:, j, 1:2]).then_inc(rs_ready, 1)
                if not final:
                    act.wait_ge(rs_ready, n + 1)
                    ACTV(xn[j][:, :], x[j][:, :], ACT.Copy, scale=rs[:, j:j + 1]).then_inc(xn_ready, 1)
                    act.wait_ge(turned, n + 1)
                    for k in range(KD // 2):
                        last = ACTV(kit.aT[:, k, bass.ds(T * P, P)], ps[j][:, k, :], ACT.Identity, scale=kit.scale1[:, cond, 1, k:k + 1],
                                    bias=kit.mcol[:, cond, 1, 0, k:k + 1])
                    last.then_inc(act_out, 1)

            tiles_of(act, step)

        @block.vector
        def _(dve):
            V = nc.vector
            TT, TS, STT = V.tensor_tensor, V.tensor_scalar, V.scalar_tensor_tensor
            ch = Chain(dve, chain_v)
            dve.wait_ge(rows_loaded, 16 * (len(groups) + (1 if final else 0)))

            def step(T, n, m, j, cond, s):
                dve.wait_ge(y_loaded[j], m * 32 + 32)
                dve.wait_ge(x_loaded[j], m * 16 + 16)
                wt = kit.wts[:, bass.ds(n, 1), :].rearrange("p a b -> p (a b)")
                ch(TS(ya[j][:, :], ya[j][:, :], wt[:, 0:1], None, ALU.mult))
                ch(STT(ya[j][:, :], yb[j][:, :], wt[:, 1:2], ya[j][:, :], ALU.mult, ALU.add))
                ch(TT(ya[j][:, :], ya[j][:, :], gate[s][:, :], ALU.mult))
                TT(x[j][:, :], x[j][:, :], ya[j][:, :], ALU.add).then_inc(h_ready, 1)
                dve.wait_ge(sq_ready, n + 1)
                ch(TS(ss[:, j, 0:1], ss[:, j, 0:1], 1.0 / D, EPS, ALU.mult, ALU.add))
                V.reciprocal(ss[:, j, 1:2], ss[:, j, 0:1]).then_inc(r_half, 1)
                if final:
                    dve.wait_ge(rs_ready, n + 1)
                    STT(xn[j][:, :], x[j][:, :], rs[:, j:j + 1], fw[:, :], ALU.mult, ALU.mult).then_inc(xn_ready, 1)
                else:
                    dve.wait_ge(turned, n + 1)
                    for k in range(KD // 2, KD):
                        last = TS(kit.aT[:, k, bass.ds(T * P, P)], ps[j][:, k, :], kit.scale1[:, cond, 1, k:k + 1],
                                  kit.mcol[:, cond, 1, 0, k:k + 1], ALU.mult, ALU.add)
                    last.then_inc(dve_out, 1)

            tiles_of(dve, step, ch, 4)

        if not final:
            @block.tensor
            def _(pe):
                def step(T, n, m, j, cond, s):
                    pe.wait_ge(xn_ready, n + 1)
                    for k in range(KD):
                        last = nc.tensor.transpose(ps[j][:, k, :], xn[j][:, k * P:(k + 1) * P], consts[:, 0:P])
                    last.then_inc(turned, 1)

                tiles_of(pe, step)


HD, HEADS, KVH = 64, 8, 2
QKV = 1536
HALF_W = 768
NR = HEADS + KVH
SCALE = HD ** -0.5
NROPE = 2 * HD // 2


def host_rope():
    rows = SEQ // 64
    row = np.repeat(np.arange(rows), 64).astype(np.float32)
    col = (np.arange(rows * 64) % 64).astype(np.float32)
    inv = (np.float32(10000.0) ** (-np.arange(0, 32, 2, dtype=np.float32) / np.float32(32))).astype(np.float32)
    ang = np.concatenate([row[:, None] * inv, col[:, None] * inv], axis=-1).astype(np.float32)
    return np.concatenate([np.cos(ang), np.sin(ang)], axis=-1).astype(np.float32)


def phase_in_odd(kit):
    nc, A, consts, aT, proj, qT, kT = kit.nc, kit.A, kit.consts, kit.aT, kit.proj, kit.qT, kit.kT
    with ExitStack() as st:
        sb = lambda n, s, d=F32: st.enter_context(nc.sbuf_tensor(f"io_{n}", s, d))
        ps = lambda n, s: st.enter_context(nc.psum_tensor(f"io_{n}", s, F32))
        w = sb("w", [P, KD, QKV])
        wn = sb("wn", [P, NR, HD])
        rope = sb("rope", [P, NT - CT, NROPE])
        sq, t1, t2 = sb("sq", [P, NR, HD]), sb("t1", [P, 2, NR, HD // 2]), sb("t2", [P, 2, NR, HD // 2])
        t3, t4 = sb("t3", [P, 2, NR, HD // 2]), sb("t4", [P, 2, NR, HD // 2])
        qrot = sb("qrot", [P, 2, 4, P])
        ss, rs = sb("ss", [P, 2, NR]), sb("rs", [P, NR])
        ps_w = [ps(f"ps_w{c}", [P, BANK]) for c in range(3)]
        ps_q = ps("ps_q", [P, 2 * 4, P])
        ps_k = ps("ps_k", [P, 2, P])
        S = lambda n: kit.sem("io_" + n)
        w_loaded, small_loaded, spare_ready = [S(f"w_loaded{c}") for c in range(3)], S("small_loaded"), S("spare_ready")
        done = [S(f"done{c}") for c in range(3)]
        taken = [S(f"taken{c}") for c in range(3)]
        r_half, rs_ready, turned_ready, q_turned, k_turned, q_taken, k_taken = (
            S(n) for n in ("r_half", "rs_ready", "turned_ready", "q_turned", "k_turned", "q_taken", "k_taken"))
        chain_v = S("chain_v")
        KV, QS, QD = range(3)
        block = st.enter_context(nc.Block())

        @block.sync
        def _(sp):
            wv = A["od_w_in"][0].rearrange("(k p) n -> p k n", p=P)
            for c, cols in ((KV, (512, 768)), (KV, (1280, 1536)), (QS, (0, 512)), (QD, (768, 1280))):
                sp.dma_start(w[:, :, cols[0]:cols[1]], wv[:, :, cols[0]:cols[1]]).then_inc(w_loaded[c], 16)
            sp.dma_start(rope[:, :, :], A["rope"].rearrange("(t p) c -> p t c", p=P)).then_inc(small_loaded, 16)
            sp.dma_start(wn[:, 0:HEADS, :], A["od_q_norm_w"].rearrange("a d -> (a d)").partition_broadcast(P).unsqueeze(1).to_broadcast([P, HEADS, HD])).then_inc(small_loaded, 16)
            sp.dma_start(wn[:, HEADS:NR, :], A["od_k_norm_w"].rearrange("a d -> (a d)").partition_broadcast(P).unsqueeze(1).to_broadcast([P, KVH, HD])).then_inc(small_loaded, 16)

        @block.gpsimd
        def _(pool):
            nc.gpsimd.memset(proj[:, NT, :], 0.0)
            nc.gpsimd.memset(kT[:, :, NT * P:(NT + 1) * P], 0.0)

        @block.tensor
        def _(pe):
            MM, TR = nc.tensor.matmul, nc.tensor.transpose

            def product(c, T, n):
                pe.wait_ge(w_loaded[c], 32 if c == KV else 16)
                if n:
                    pe.wait_ge(taken[c], n)
                for k in range(KD):
                    lhsT = aT[:, k, T * P:(T + 1) * P]
                    if c == KV:
                        last = MM(ps_w[c][:, :].rearrange("p (a n) -> p a n", a=2), lhsT,
                                  w[:, k, :].rearrange("p (a n) -> p a n", a=2)[:, :, 512:768], start=(k == 0), stop=(k == KD - 1))
                    else:
                        at = 0 if c == QS else HALF_W
                        last = MM(ps_w[c][:, :], lhsT, w[:, k, at:at + 512], start=(k == 0), stop=(k == KD - 1))
                last.then_inc(done[c], 1)

            def turn(T):
                pe.wait_ge(turned_ready, T + 1)
                if T:
                    pe.wait_ge(k_taken, T)
                for half in range(2):
                    last = TR(ps_k[:, half, :], proj[:, T, half * HALF_W + 512:half * HALF_W + 640], consts[:, 0:P])
                last.then_inc(k_turned, 1)
                if T >= CT:
                    if T > CT:
                        pe.wait_ge(q_taken, T - CT)
                    for half in range(2):
                        for j in range(4):
                            last = TR(ps_q[:, half * 4 + j, :], qrot[:, half, j, :], consts[:, 0:P])
                    last.then_inc(q_turned, 1)

            for T in range(NT):
                product(KV, T, T)
                if T >= CT:
                    product(QS, T, T - CT)
                    product(QD, T, T - CT)
                if T:
                    turn(T - 1)
            turn(NT - 1)

        @block.scalar
        def _(act):
            for T in range(NT):
                act.wait_ge(done[KV], T + 1)
                nc.scalar.copy(proj[:, T, :].rearrange("p (a n) -> p a n", a=2)[:, :, 512:768], ps_w[KV][:, :].rearrange("p (a n) -> p a n", a=2)).then_inc(taken[KV], 1)
                if T >= CT:
                    for c, at in ((QS, 0), (QD, HALF_W)):
                        act.wait_ge(done[c], T - CT + 1)
                        nc.scalar.copy(proj[:, T, at:at + 512], ps_w[c][:, :]).then_inc(taken[c], 1)
                act.wait_ge(r_half, T + 1)
                h0 = 0 if T >= CT else HEADS
                nc.scalar.sqrt(rs[:, h0:NR], ss[:, 1, h0:NR]).then_inc(rs_ready, 1)
                if T > CT:
                    act.wait_ge(q_turned, T - CT)
                    nc.scalar.copy(qT[:, T - 1 - CT, :, :], ps_q[:, :, :]).then_inc(q_taken, 1)
            act.wait_ge(q_turned, NT - CT)
            nc.scalar.copy(qT[:, NT - 1 - CT, :, :], ps_q[:, :, :]).then_inc(q_taken, 1)

        @block.vector
        def _(dve):
            V = nc.vector
            TT, TS = V.tensor_tensor, V.tensor_scalar
            ch = Chain(dve, chain_v)
            dve.wait_ge(small_loaded, 48)

            def take_k(T):
                dve.wait_ge(k_turned, T + 1)
                V.tensor_copy(kT[:, :, T * P:(T + 1) * P], ps_k[:, :, :]).then_inc(k_taken, 1)

            for T in range(NT):
                h0 = 0 if T >= CT else HEADS
                n = NR - h0
                x = proj[:, T, HALF_W:HALF_W + NR * HD].rearrange("p (h x) -> p h x", x=HD)[:, h0:NR, :]
                dve.wait_ge(taken[KV], T + 1)
                if T >= CT:
                    dve.wait_ge(taken[QD], T - CT + 1)
                    dve.wait_ge(taken[QS], T - CT + 1)
                ch(TT(sq[:, h0:NR, :], x, x, ALU.mult))
                ch(V.tensor_reduce(ss[:, 0, h0:NR], sq[:, h0:NR, :], AX.X, ALU.add))
                ch(TS(ss[:, 0, h0:NR], ss[:, 0, h0:NR], 1.0 / HD, EPS, ALU.mult, ALU.add))
                V.reciprocal(ss[:, 1, h0:NR], ss[:, 0, h0:NR]).then_inc(r_half, 1)
                if T:
                    take_k(T - 1)
                dve.wait_ge(rs_ready, T + 1)
                ch(TT(x, x, rs[:, h0:NR].unsqueeze(2).to_broadcast([P, n, HD]), ALU.mult))
                last = TT(x, x, wn[:, h0:NR, :], ALU.mult)
                if T >= CT:
                    ch(last)
                    t = T - CT
                    pairs = proj[:, T, :].rearrange("p (a n) -> p a n", a=2)[:, :, 0:NR * HD].rearrange("p a (h x two) -> p a h x two", h=NR, two=2)
                    x1, x2 = pairs[:, :, :, :, 0], pairs[:, :, :, :, 1]
                    cs, sn = (rope[:, t, c * 32:c * 32 + 32].unsqueeze(1).to_broadcast([P, NR, 32]) for c in range(2))
                    for half in range(2):
                        for dst, src, tab in ((t1, x1, cs), (t2, x2, sn), (t3, x1, sn), (t4, x2, cs)):
                            last = TT(dst[:, half], src[:, half], tab, ALU.mult)
                    ch(last)
                    ks = slice(HEADS, NR)
                    TT(x1[:, :, ks], t1[:, :, ks], t2[:, :, ks], ALU.subtract)
                    TT(x2[:, :, ks], t3[:, :, ks], t4[:, :, ks], ALU.add)
                    if t:
                        dve.wait_ge(q_turned, t)
                    for half in range(2):
                        for two, (a, b), op in ((0, (t1, t2), ALU.subtract), (1, (t3, t4), ALU.add)):
                            dst = qrot[:, half].rearrange("p j (u x two) -> p u j x two", u=2, two=2)[:, :, :, :, two]
                            a, b = (z[:, half, 0:HEADS].rearrange("p (u j) x -> p u j x", u=2) for z in (a, b))
                            last = TT(dst, a, b, op)
                last.then_inc(turned_ready, 1)
            take_k(NT - 1)


def phase_attention(kit):
    nc, A, consts, proj, qT, kT = kit.nc, kit.A, kit.consts, kit.proj, kit.qT, kit.kT
    NQ = NT - CT
    GROUPS = [(kind, j) for kind in range(2) for j in range(4)]
    NG = len(GROUPS)
    KEYS = (CTX + 3 * P, TOK)
    BANKS = (0, 1, 2, 0)
    with ExitStack() as st:
        sb = lambda n, s, d=F32: st.enter_context(nc.sbuf_tensor(f"at_{n}", s, d))
        ps = lambda n, s: st.enter_context(nc.psum_tensor(f"at_{n}", s, F32))
        mask = sb("mask", [P, NQ, KEYS[0]])
        qs, kwin = sb("qs", [P, NG, P]), sb("kwin", [P, 3 * P])
        sc = [[sb(f"sc{b}{u}", [P, TOK]) for u in range(2)] for b in range(2)]
        pT = [[sb(f"pT{b}{u}", [P, TOK]) for u in range(2)] for b in range(2)]
        sink, sink8 = sb("sink", [P, 2, 4]), sb("sink8", [P, 2, 4])
        mx, neg, rsum, es, rec = (sb(n, [P, 2, 2]) for n in ("mx", "neg", "rsum", "es", "rec"))
        ps_s = [ps(f"ps_s{u}", [P, 2 * BANK]) for u in range(2)]
        ps_t = [ps(f"ps_t{b}", [P, BANK]) for b in range(3)]
        ps_o = ps("ps_o", [P, BANK])
        S = lambda n: kit.sem("at_" + n)
        sink_loaded, sink_ready, mask_ready, q_ready, q_used = (S(n) for n in ("sink_loaded", "sink_ready", "mask_ready", "q_ready", "q_used"))
        s_ready, max_ready, neg_ready, p_ready, t_ready, o_ready, o_taken = (
            S(n) for n in ("s_ready", "max_ready", "neg_ready", "p_ready", "t_ready", "o_ready", "o_taken"))
        t_act, t_dve = S("t_act"), S("t_dve")
        chain_v = S("chain_v")
        block = st.enter_context(nc.Block())

        def tiles(kind, h):
            n = KEYS[kind] // P
            return range(0, 3) if h == 0 else range(3, n)

        @block.sync
        def _(sp):
            sp.dma_start(sink[:, :, :].rearrange("p u j -> p (u j)"), A["od_sink"].rearrange("a h -> (a h)").partition_broadcast(P)).then_inc(sink_loaded, 16)

        @block.gpsimd
        def _(pool):
            G = nc.gpsimd
            G.memset(mask[:, :, :], 0.0).then_inc(mask_ready, 1)
            pool.wait_ge(mask_ready, 1)
            for i in range(NQ):
                left, right = mask[:, i, CTX:CTX + P], mask[:, i, CTX + 2 * P:CTX + 3 * P]
                last = G.memset(left, NEG) if i == 0 else G.tensor_copy(left, consts[:, C_NGE:C_NGE + P])
                last = G.memset(right, NEG) if i == NQ - 1 else G.tensor_copy(right, consts[:, C_NLE:C_NLE + P])
            last.then_inc(mask_ready, 1)
            pool.sem_inc(q_used, 1)
            with pool.Fori(0, NQ) as i:
                pool.wait_ge(q_used, i + 1)
                G.tensor_copy(kwin[:, :], kT[:, 0, bass.ds(i * P + P, 3 * P)])
                G.tensor_copy(qs[:, :, :].rearrange("p g q -> p (g q)"), qT[:, bass.ds(i, 1), :, :].rearrange("p a g q -> p (a g q)")).then_inc(q_ready, 1)

        @block.tensor
        def _(pe):
            MM, TR = nc.tensor.matmul, nc.tensor.transpose

            def scores(i, g):
                kind, j = GROUPS[g]
                base = i * NG
                if g == 0:
                    pe.wait_ge(q_ready, i + 1)
                pe.wait_ge(p_ready, (base + g) * 2 + 2)
                keys = kT[:, 0, 0:CTX], kwin[:, 0:CTX], kwin[:, CTX:3 * P]
                parts = [(0, BANK, kT[:, 1, 0:BANK]), (BANK, TOK, kT[:, 1, BANK:TOK])] if kind == 1 else [
                    (0, CTX, keys[0]), (CTX, BANK, keys[1]), (BANK, KEYS[0], keys[2])]
                for a, b, key in parts:
                    for u in range(2):
                        rows = slice(u * HD, (u + 1) * HD)
                        last = MM(ps_s[u][:, a:b], qs[rows, g, :], key[rows, :], start=True, stop=True)
                last.then_inc(s_ready, 1)
                if g == NG - 1:
                    pe.wait_ge(s_ready, base + g + 1)
                    pe.sem_inc(q_used, 1)

            def weigh(i, g):
                kind, j = GROUPS[g]
                n = i * NG + g
                for u in range(2):
                    pe.wait_ge(p_ready, n * 2 + u + 3)
                    for h in range(2):
                        at = (g * 4 + u * 2 + h) % 4
                        bank = BANKS[at]
                        if at == 3:
                            pe.wait_ge(t_act, n * 2 + 2)
                        elif at == 0:
                            pe.wait_ge(t_dve, n * 2 + 1)
                        for m, t in enumerate(tiles(kind, h)):
                            last = TR(ps_t[bank][:, m * P:(m + 1) * P], sc[g % 2][u][:, t * P:(t + 1) * P], consts[:, 0:P])
                        last.then_inc(t_ready, 1)
                pe.wait_ge(o_taken, n + 1)
                nk = KEYS[kind] // P
                for u in range(2):
                    pe.wait_ge(t_act, n * 2 + u + 2)
                    pe.wait_ge(t_dve, n * 2 + u + 2)
                    for t in range(nk):
                        vcols = slice(kind * HALF_W + 640 + u * HD, kind * HALF_W + 640 + (u + 1) * HD)
                        T = t if kind == 1 or t < CT else i + (t - CT + 1)
                        v = proj[:, T, vcols] if isinstance(T, int) else proj[:, bass.ds(T, 1), vcols].rearrange("p a x -> p (a x)")
                        last = MM(ps_o[:, u * HD:(u + 1) * HD], pT[g % 2][u][:, t * P:(t + 1) * P], v, start=(t == 0), stop=(t == nk - 1))
                last.then_inc(o_ready, 1)

            with pe.Fori(0, NQ) as i:
                scores(i, 0)
                for g in range(NG):
                    if g + 1 < NG:
                        scores(i, g + 1)
                    weigh(i, g)

        @block.scalar
        def _(act):
            act.sem_inc(p_ready, 1)
            act.sem_inc(p_ready, 1)
            act.sem_inc(t_act, 1)
            ACTV = nc.scalar.activation

            def soften(i, g):
                kind, j = GROUPS[g]
                n, b = i * NG + g, g % 2
                act.wait_ge(neg_ready, n + 1)
                for u in range(2):
                    src = ps_s[u] if kind == 1 else sc[b][u]
                    if kind == 0:
                        ACTV(es[:, b, u:u + 1], sink[:, u, j:j + 1], ACT.Exp, bias=neg[:, b, u:u + 1])
                    ACTV(sc[b][u][:, 0:KEYS[kind]], src[:, 0:KEYS[kind]], ACT.Exp, scale=SCALE, bias=neg[:, b, u:u + 1],
                         accum_out=rsum[:, b, u:u + 1]).then_inc(p_ready, 1)

            def copy(i, g):
                n = i * NG + g
                for u in range(2):
                    act.wait_ge(t_ready, n * 4 + u * 2 + 1)
                    bank = BANKS[u * 2]
                    nc.scalar.copy(pT[g % 2][u][:, 0:3 * P], ps_t[bank][:, 0:3 * P]).then_inc(t_act, 1)

            with act.Fori(0, NQ) as i:
                soften(i, 0)
                for g in range(NG):
                    copy(i, g)
                    if g + 1 < NG:
                        soften(i, g + 1)

        @block.vector
        def _(dve):
            V = nc.vector
            TT, TS = V.tensor_tensor, V.tensor_scalar
            ch = Chain(dve, chain_v)
            dve.sem_inc(t_dve, 1)
            dve.sem_inc(o_taken, 1)
            dve.wait_ge(sink_loaded, 16)
            dve.wait_ge(mask_ready, 2)
            ch(TS(sink8[:, :, :], sink[:, :, :], 1.0 / SCALE, None, ALU.mult))

            def largest(i, g, u):
                kind, j = GROUPS[g]
                n, b = i * NG + g, g % 2
                dve.wait_ge(s_ready, n + 1)
                if kind == 0:
                    ch(TT(sc[b][u][:, 0:KEYS[0]], ps_s[u][:, 0:KEYS[0]], mask[:, bass.ds(i, 1), :].rearrange("p a k -> p (a k)"), ALU.add))
                    ch(V.tensor_reduce(mx[:, b, u:u + 1], sc[b][u][:, 0:KEYS[0]], AX.X, ALU.max))
                else:
                    ch(V.tensor_reduce(mx[:, b, u:u + 1], ps_s[u][:, 0:KEYS[1]], AX.X, ALU.max))
                if u == 1:
                    if kind == 0:
                        ch(TT(mx[:, b, :], mx[:, b, :], sink8[:, :, j], ALU.max))
                    TS(neg[:, b, :], mx[:, b, :], -SCALE, None, ALU.mult).then_inc(neg_ready, 1)

            def copy(i, g, u):
                kind, j = GROUPS[g]
                n = i * NG + g
                dve.wait_ge(t_ready, n * 4 + u * 2 + 2)
                w = len(tiles(kind, 1)) * P
                V.tensor_copy(pT[g % 2][u][:, 3 * P:3 * P + w], ps_t[BANKS[u * 2 + 1]][:, 0:w]).then_inc(t_dve, 1)

            def normalise(i, g):
                kind, j = GROUPS[g]
                n, b = i * NG + g, g % 2
                if kind == 0:
                    ch(TT(rsum[:, b, :], rsum[:, b, :], es[:, b, :], ALU.add))
                ch(V.reciprocal(rec[:, b, :], rsum[:, b, :]))
                dve.wait_ge(o_ready, n + 1)
                at = kind * 512
                dst = kit.yacc[:, bass.ds(i + CT, 1), at:at + 512].rearrange("p a (u j x) -> p (a u) j x", u=2, j=4)[:, :, j, :]
                TT(dst, ps_o[:, 0:2 * HD].rearrange("p (u x) -> p u x", u=2), rec[:, b, :].unsqueeze(2).to_broadcast([P, 2, HD]), ALU.mult).then_inc(o_taken, 1)

            with dve.Fori(0, NQ) as i:
                ch.enter(i, 4 * 7 + 4 * 3)
                largest(i, 0, 0)
                largest(i, 0, 1)
                for g in range(NG):
                    for u in range(2):
                        if g + 1 < NG:
                            largest(i, g + 1, u)
                        copy(i, g, u)
                    normalise(i, g)
                ch.leave(NQ)


def program(nc, A, out):
    with ExitStack() as stack:
        kit = Kit(nc, A, out, stack)
        kit.mod = kit.dram("mod", [2, DEPTH * 6 * D])
        kit.feat, kit.tokc, kit.zvo = kit.dram("feat", [NCH, P, TOK]), kit.dram("tokc", [TOK, CONV_CH]), kit.dram("zvo", [TOK, ZVO])
        kit.ac_rows, kit.M_rows = kit.dram("ac_rows", [NDT, TOK]), kit.dram("M_rows", [NML, TOK])
        kit.cd_rows, kit.sd_rows = kit.dram("cd_rows", [NDT, NT]), kit.dram("sd_rows", [NML, NT])
        kit.h_mid, kit.h_next, kit.t = (kit.dram(n, [TOK, D]) for n in ("h_mid", "h_next", "t"))
        kit.y, kit.slot_tok = kit.dram("y", [MAXCH * P, D]), kit.dram("slot_tok", [NCK * P, 1], I32)
        kit.logits, kit.wts = kit.keep("logits", [P, NT, 20]), kit.keep("wts", [P, NT, 2])
        kit.pos, kit.plan = kit.keep("pos", [P, NT, 2], I32), kit.keep("plan", [P, NCK + 1], I32)
        kit.slots_in = kit.keep("slots_in", [P, NCK], I32)

        def hold(scope, name, shape):
            return scope.enter_context(nc.sbuf_tensor(name, shape, F32))

        with ExitStack() as scope:
            kit.tokS, kit.tokM = hold(scope, "tokS", [P, NT, P]), hold(scope, "tokM", [P, NT, P])
            with ExitStack() as inner:
                kit.aT = hold(inner, "aT_even", [P, KD, TOK])
                phase_adaln(kit)
                phase_columns(kit)
                phase_norm_in(kit, 0, [(A["ctx"][0], 0, CT, 1), (A["x"][0], CT, NT - CT, 0)])
                phase_in_even(kit)
            kit.yacc, kit.hacc = hold(scope, "yacc_even", [P, NT + 1, D]), hold(scope, "hacc", [P, NT + 1, D])
            phase_recurrent(kit)
            phase_out(kit, 0, [(A["ctx"][0], 0, CT, 1), (A["x"][0], CT, NT - CT, 0)], A["ev_w_out"][0], 2 * KD, kit.h_mid)
        kit.recycle()
        with ExitStack() as scope:
            kit.yacc = hold(scope, "yacc_odd", [P, NT, D])
            with ExitStack() as inner:
                kit.proj, kit.qT, kit.kT = (hold(inner, n, s) for n, s in (("proj", [P, NT + 1, QKV]), ("qT", [P, NT - CT, KD, P]), ("kT", [P, 2, (NT + 1) * P])))
                with ExitStack() as innermost:
                    kit.aT = hold(innermost, "aT_odd", [P, KD, TOK])
                    phase_route(kit, 0, 0, NT)
                    phase_experts(kit, 0, NT)
                    phase_combine(kit, 0, kit.h_mid, kit.h_next, [(0, CT, 1), (CT, NT - CT, 0)], False)
                    phase_in_odd(kit)
                phase_attention(kit)
            phase_out(kit, 1, [(kit.h_next[CTX:TOK, :], CT, NT - CT, 0)], A["od_w_out"][0], KD, kit.h_mid)
        kit.recycle()
        phase_route(kit, 1, CT, NT - CT)
        phase_experts(kit, 1, NT - CT)
        phase_combine(kit, 1, kit.h_mid, None, [(CT, NT - CT, 0)], True)


_INS = ["x", "c", "ctx", "c_ctx", "ada_w", "ada_b", "norm1_w", "norm2_w", "ev_w_in", "ev_conv_w", "ev_conv_b", "ev_dt_bias",
        "ev_a_log", "ev_d_skip", "ev_ssd_norm_w", "ev_ig_bias", "ev_fg_bias", "ev_mlstm_norm_w", "ev_w_out", "od_w_in", "od_sink",
        "od_q_norm_w", "od_k_norm_w", "od_w_out", "moe_w_group", "moe_w_expert", "moe_w_gate", "moe_w_up", "moe_w_down", "final_norm_w"]


def kernel(**inputs):
    import numpy as _np
    import concourse.bacc as _bacc
    from concourse import mybir as _mybir
    from concourse.bass_utils import run_bass_kernel_spmd as _run

    nc = _bacc.Bacc("TRN2", target_bir_lowering=False, num_devices=1)
    arrays, A = {}, {}
    tables = {"consts": host_consts(), "route": host_route(), "rope": host_rope()}
    for name in _INS + list(tables):
        a = tables[name] if name in tables else _np.ascontiguousarray(inputs[name])
        arrays[f"in_{name}_dram"] = a
        A[name] = nc.dram_tensor(f"in_{name}_dram", a.shape, _mybir.dt.from_np(a.dtype), kind="ExternalInput").ap()
    out = nc.dram_tensor("out_0_dram", (1, SEQ, D), F32, kind="ExternalOutput").ap()
    program(nc, A, out)
    r = _run(nc, [arrays], core_ids=[0])
    return r.results[0]["out_0_dram"]
```
